# Optimizing a Trainium2 kernel written in Bass

```python
import jax, jax.numpy as jnp
from jax import lax
import numpy as np

D_MODEL = 1024
BATCH = 1
SEQ = 256
DEPTH = 2
DEC_BATCH = 8
DEC_SEQ = 4
PAST_LEN = 2048
PAGE_SIZE = 128

CHUNK = 128
N_GROUPS_A = 8
D_A = 1024
GROUP_A = D_A // N_GROUPS_A
D_B = 1024
CONV_W = 3
D_PLE = 256
N_KEYS = 128
N_EXPERTS = N_KEYS * N_KEYS
PEER_HEADS = 8
D_QUERY = 256
D_HALF = D_QUERY // 2
TOPK = 16
PEER_BLOCK = 256
EPS = 1e-6
D_IN = 2 * D_A + 3 * D_B + 2 * D_MODEL

kernel_name = 'hybrid_gmlp_shortconv_peer_decoder_step'

def _rmsnorm(x, g):
    xf = x.astype(jnp.float32)
    y = xf * lax.rsqrt(jnp.mean(xf * xf, axis=-1, keepdims=True) + EPS)
    return (y * g.astype(jnp.float32)).astype(x.dtype)

def _chunk_gmlp(u, v, w_s, b_s):
    bsz, L, _ = v.shape
    n_chunks = -(-L // CHUNK)
    pad = n_chunks * CHUNK - L
    vp = jnp.pad(v, ((0, 0), (0, pad), (0, 0)))
    vc = vp.reshape(bsz, n_chunks, CHUNK, N_GROUPS_A, GROUP_A)
    mask = jnp.tril(jnp.ones((CHUNK, CHUNK), dtype=bool))
    w = jnp.where(mask[None], w_s, jnp.zeros_like(w_s))
    s = jnp.einsum('gts,bcsgd->bctgd', w, vc) + b_s.T[None, None, :, :, None]
    s = s.reshape(bsz, n_chunks * CHUNK, D_A)[:, :L]
    return u * s

def _short_conv(xc, prev, conv_w):
    L = xc.shape[1]
    xp = jnp.concatenate([prev.astype(xc.dtype), xc], axis=1)
    y = conv_w[0] * xp[:, :L] + conv_w[1] * xp[:, 1:L + 1] + conv_w[2] * xp[:, 2:]
    return y, xp[:, L:]

def _peer(h, w_q, k1, k2, u_tab, v_tab):
    bsz, L, d = h.shape
    T = bsz * L
    nb = -(-T // PEER_BLOCK)
    hf = jnp.pad(h.reshape(T, d), ((0, nb * PEER_BLOCK - T), (0, 0)))
    hb = hf.reshape(nb, PEER_BLOCK, d)

    def block_fn(xb):
        q = (xb @ w_q).reshape(PEER_BLOCK, PEER_HEADS, D_QUERY)
        s1 = jnp.einsum('thd,kd->thk', q[..., :D_HALF], k1).astype(jnp.float32)
        s2 = jnp.einsum('thd,kd->thk', q[..., D_HALF:], k2).astype(jnp.float32)
        t1, i1 = lax.top_k(s1, TOPK)
        t2, i2 = lax.top_k(s2, TOPK)
        cand = (t1[..., :, None] + t2[..., None, :]).reshape(PEER_BLOCK, PEER_HEADS, TOPK * TOPK)
        ts, ic = lax.top_k(cand, TOPK)
        e1 = jnp.take_along_axis(i1, ic // TOPK, axis=-1)
        e2 = jnp.take_along_axis(i2, ic % TOPK, axis=-1)
        eid = e1 * N_KEYS + e2
        g = jax.nn.softmax(ts, axis=-1)
        ue = u_tab[eid]
        a = jax.nn.gelu(jnp.einsum('thkd,td->thk', ue, xb).astype(jnp.float32))
        ve = v_tab[eid]
        return jnp.einsum('thk,thkd->td', (g * a).astype(xb.dtype), ve)

    out = lax.map(block_fn, hb).reshape(nb * PEER_BLOCK, d)[:T]
    return out.reshape(bsz, L, d)

def _layer(x, pe, conv_prev, ln1, w_in, ln_v, w_s, b_s, conv_w, w_a, w_b, w_o,
           ln2, w_q, k1, k2, u_tab, v_tab, ln3, w_pg, w_ple):
    h = _rmsnorm(x, ln1)
    z = h @ w_in
    idx = [D_A, 2 * D_A, 2 * D_A + D_B, 2 * D_A + 2 * D_B, 2 * D_A + 3 * D_B,
           2 * D_A + 3 * D_B + D_MODEL]
    u, v, bg, cg, xin, ga, gb = jnp.split(z, idx, axis=-1)
    u = jax.nn.gelu(u)
    v = _rmsnorm(jax.nn.gelu(v), ln_v)
    ya = _chunk_gmlp(u, v, w_s, b_s) @ w_a
    yc, conv_new = _short_conv(cg * xin, conv_prev, conv_w)
    yb = (bg * yc) @ w_b
    x = x + (jax.nn.sigmoid(ga) * ya + jax.nn.sigmoid(gb) * yb) @ w_o
    x = x + _peer(_rmsnorm(x, ln2), w_q, k1, k2, u_tab, v_tab)
    x = x + jax.nn.sigmoid(_rmsnorm(x, ln3) @ w_pg) * (pe @ w_ple)
    return x, v, conv_new

def setup_inputs(seed: int = 0) -> dict:
    key = jax.random.key(seed)
    ks = jax.random.split(key, 32)
    f32 = jnp.float32
    nrm = lambda k, s, sc: (jax.random.normal(k, s, f32) * sc).astype(f32)
    gain = lambda k, s: 1.0 + 0.02 * jax.random.normal(k, s, f32)
    return {
        'x_prompt': nrm(ks[0], (BATCH, SEQ, D_MODEL), 1.0),
        'x_sample': nrm(ks[1], (DEC_BATCH, DEC_SEQ, D_MODEL), 1.0),
        'state_conv': nrm(ks[2], (DEPTH, DEC_BATCH, CONV_W - 1, D_B), 1.0),
        'p_prompt': nrm(ks[3], (DEPTH, BATCH, SEQ, D_PLE), 1.0),
        'p_sample': nrm(ks[4], (DEPTH, DEC_BATCH, DEC_SEQ, D_PLE), 1.0),
        'ln1': gain(ks[5], (DEPTH, D_MODEL)),
        'w_in': nrm(ks[6], (DEPTH, D_MODEL, D_IN), D_MODEL ** -0.5),
        'ln_v': gain(ks[7], (DEPTH, D_A)),
        'w_s': nrm(ks[8], (DEPTH, N_GROUPS_A, CHUNK, CHUNK), CHUNK ** -0.5),
        'b_s': gain(ks[9], (DEPTH, N_GROUPS_A, CHUNK)),
        'conv_w': nrm(ks[10], (DEPTH, CONV_W, D_B), CONV_W ** -0.5),
        'w_a': nrm(ks[11], (DEPTH, D_A, D_MODEL), D_A ** -0.5),
        'w_b': nrm(ks[12], (DEPTH, D_B, D_MODEL), D_B ** -0.5),
        'w_o': nrm(ks[13], (DEPTH, D_MODEL, D_MODEL), D_MODEL ** -0.5),
        'ln2': gain(ks[14], (DEPTH, D_MODEL)),
        'w_q': nrm(ks[15], (DEPTH, D_MODEL, PEER_HEADS * D_QUERY), D_MODEL ** -0.5),
        'k1': nrm(ks[16], (DEPTH, N_KEYS, D_HALF), D_HALF ** -0.5),
        'k2': nrm(ks[17], (DEPTH, N_KEYS, D_HALF), D_HALF ** -0.5),
        'u_tab': nrm(ks[18], (DEPTH, N_EXPERTS, D_MODEL), D_MODEL ** -0.5),
        'v_tab': nrm(ks[19], (DEPTH, N_EXPERTS, D_MODEL), PEER_HEADS ** -0.5),
        'ln3': gain(ks[20], (DEPTH, D_MODEL)),
        'w_pg': nrm(ks[21], (DEPTH, D_MODEL, D_MODEL), D_MODEL ** -0.5),
        'w_ple': nrm(ks[22], (DEPTH, D_PLE, D_MODEL), D_PLE ** -0.5),
        'ln_f': gain(ks[23], (D_MODEL,)),
    }

def reference(x_prompt, x_sample, state_conv, p_prompt, p_sample, ln1, w_in, ln_v,
              w_s, b_s, conv_w, w_a, w_b, w_o, ln2, w_q, k1, k2, u_tab, v_tab,
              ln3, w_pg, w_ple, ln_f):
    conv_p0 = jnp.zeros((x_prompt.shape[0], CONV_W - 1, D_B), x_prompt.dtype)
    xp, xs = x_prompt, x_sample
    conv_prompt, conv_sample, v_sample = [], [], []
    for i in range(DEPTH):
        lp = (ln1[i], w_in[i], ln_v[i], w_s[i], b_s[i], conv_w[i], w_a[i], w_b[i], w_o[i],
              ln2[i], w_q[i], k1[i], k2[i], u_tab[i], v_tab[i], ln3[i], w_pg[i], w_ple[i])
        xp, _, cp = _layer(xp, p_prompt[i], conv_p0, *lp)
        xs, vs, cs = _layer(xs, p_sample[i], state_conv[i], *lp)
        conv_prompt.append(cp)
        conv_sample.append(cs)
        v_sample.append(vs)
    y_prompt = _rmsnorm(xp, ln_f)
    y_sample = _rmsnorm(xs, ln_f)
    return (y_prompt, y_sample, jnp.stack(conv_prompt), jnp.stack(conv_sample), jnp.stack(v_sample))


_drawn_inputs = setup_inputs


def setup_inputs(seed=0):
    import zlib

    import numpy as np

    out = dict(_drawn_inputs(seed))
    spreads = {}
    factors = {'ln3': 19.532, 'ln_f': 8.435}
    for name, (base, spread) in spreads.items():
        noise = np.random.default_rng([zlib.crc32(name.encode()), seed]).standard_normal(out[name].shape)
        drawn = base * np.exp(spread * noise) if base else spread * noise
        out[name] = __import__('jax').numpy.asarray(drawn.astype(out[name].dtype))
    for name, factor in factors.items():
        out[name] = (out[name] * factor).astype(out[name].dtype)
    return out
```

```python
import concourse.bass as bass
from concourse import mybir
from contextlib import ExitStack

P = 128
DEPTH = 2
D = 1024
C = D // P
SEQ, DEC_B, DEC_S = 256, 8, 4
DEC = DEC_B * DEC_S
T = SEQ + DEC
CHUNK = 128
GROUPS = 8
HEADS = 8
KEYS = 128
TOPK = 16
D_PLE = 256
CP = D_PLE // P
EPS = 1e-6
TT = 96
NT = T // TT
ROUTES = NT * HEADS
EXT = 2 + SEQ + DEC_B * (2 + DEC_S)

SEGS = ["v", "u", "c", "x", "b", "ga", "gb"]
Q_IN = 0
Q_A = 14
Q_B = 16
Q_O = 18
Q_Q = 20
Q_U = 24
Q_V = Q_U + KEYS // 4
Q_PG = Q_V + KEYS // 4
Q_PLE = Q_PG + 2
QUADS = Q_PLE + 1
UNITS = 4 * QUADS
U_TOP = 12
U_ONLY = 2
U_MIX = KEYS // 4 - U_TOP - U_ONLY
E_MIX = 4 * (U_TOP + U_ONLY)
EVACS = UNITS - KEYS
NORMS = 4
PREPS = 7

F32 = mybir.dt.float32
F32R = mybir.dt.float32r
U32 = mybir.dt.uint32
ALU = mybir.AluOpType
ACT = mybir.ActivationFunctionType
AX = mybir.AxisListType
LOWEST = -3.0e38


def hybrid_trunk(nc, stream, x_in, pe_in, conv_in, gains_in, ws_in, ws_blk_in, bias_in, keys_in,
                 y_out, conv_out, v_out):
    ctx = ExitStack()
    with ctx:
        def sb(name, shape, dt, where=ctx):
            return where.enter_context(nc.sbuf_tensor(name, shape, dt))

        def sem(name):
            return ctx.enter_context(nc.semaphore(name))

        raw = sb("raw", [P, 4, D], F32)
        w_hi = sb("w_hi", [P, 2, D], F32R)
        w_lo = sb("w_lo", [P, 2, D], F32R)
        h_hi = sb("h_hi", [P, C, T], F32R)
        h_lo = sb("h_lo", [P, C, T], F32R)
        gains = sb("gains", [P, DEPTH, 8, C], F32)
        iota = sb("iota", [P, P], F32)
        ident = sb("ident", [P, P], F32)
        ones = sb("ones", [P, P], F32)
        eps = sb("eps", [P, 1], F32)
        routeT = sb("routeT", [P, 3, T], F32)
        hot1 = sb("hot1", [P, 4, P], F32)
        hot2 = sb("hot2", [P, 4, P], F32)
        act_u = sb("act_u", [P, 2, T], F32)

        front = ExitStack()
        x = sb("x", [P, C, T], F32, front)
        z = sb("z", [P, 7 * C, T], F32, front)
        t_op = sb("t_op", [P, C, T], F32, front)
        b_hi = sb("b_hi", [P, C, T], F32R, front)
        b_lo = sb("b_lo", [P, C, T], F32R, front)
        ext = sb("ext", [P, C, EXT], F32, front)
        root = sb("root", [P, T], F32, front)
        mixer = ExitStack()
        v_tok = sb("v_tok", [P, 3, D], F32, mixer)
        ws = sb("ws", [P, GROUPS, CHUNK], F32, mixer)
        ws_blk = sb("ws_blk", [DEC, GROUPS, DEC], F32, mixer)
        bias = sb("bias", [1, GROUPS, T], F32, mixer)
        prev = sb("prev", [P, C, DEC_B, 2], F32, mixer)
        after = sb("after", [P, C, 2 + 2 * DEC_B], F32, mixer)
        mixer.close()
        routing = ExitStack()
        scores = sb("scores", [TT, ROUTES, 2, KEYS], F32, routing)
        row = sb("row", [TT, 2, KEYS], F32, routing)
        top = sb("top", [TT, TOPK], F32, routing)
        cut = sb("cut", [TT, 2, KEYS], F32, routing)
        cand = sb("cand", [TT, TOPK, TOPK], F32, routing)
        cand2 = sb("cand2", [TT, TOPK, TOPK], F32, routing)
        hit = sb("hit", [TT, 2, TOPK, TOPK], F32, routing)
        best = sb("best", [TT, 2, TOPK], F32, routing)
        besti = sb("besti", [TT, 2, TOPK], U32, routing)
        bestf = sb("bestf", [TT, 2, TOPK], F32, routing)
        pick = sb("pick", [TT, TOPK], U32, routing)
        pick2 = sb("pick2", [TT, 2, TOPK], U32, routing)
        pickf = sb("pickf", [TT, 2, TOPK], F32, routing)
        route = sb("route", [TT, 3, ROUTES, TOPK], F32, routing)
        total = sb("total", [TT, ROUTES], F32, routing)
        keys = sb("keys", [P, 2, KEYS], F32, routing)
        routing.close()
        front.close()
        mat = sb("mat", [P, KEYS, T], F32)
        sq = ext[:, :, 0:T]

        ps = ctx.enter_context(nc.psum_tensor("ps", [P, 8, 512], F32))
        x_keep = nc.dram_tensor("x_keep", (P, C * T), F32, kind="Internal").ap()

        raw_in = [sem(f"raw_in{j}") for j in range(4)]
        hi = sem("hi")
        lo = sem("lo")
        mm = sem("mm")
        evac = sem("evac")
        passed = sem("passed")
        const_dve = sem("const_dve")
        const_pool = sem("const_pool")
        gains_got = sem("gains_got")
        x_got = sem("x_got")
        conv_got = sem("conv_got")
        mixw_got = sem("mixw_got")
        mixw_ok = sem("mixw_ok")
        pe_got = sem("pe_got")
        keys_got = sem("keys_got")
        kept = sem("kept")
        back = sem("back")
        out_v = sem("out_v")
        out_c = sem("out_c")
        out_y = sem("out_y")
        sq_ok = sem("sq_ok")
        ss_ok = sem("ss_ok")
        rt_ok = sem("rt_ok")
        nt_ok = sem("nt_ok")
        ab_ok = sem("ab_ok")
        mix_ok = sem("mix_ok")
        op_hi = sem("op_hi")
        op_lo = sem("op_lo")
        tr_ok = sem("tr_ok")
        tok_ok = sem("tok_ok")
        s_ok = sem("s_ok")
        s_used = sem("s_used")
        x_new = sem("x_new")
        cx_ok = sem("cx_ok")
        sc_ok = sem("sc_ok")
        sc_in = sem("sc_in")
        top_ok = sem("top_ok")
        ex_ok = sem("ex_ok")
        rt_w = sem("rt_w")
        rT_ok = sem("rT_ok")
        rT_in = sem("rT_in")
        one_ok = sem("one_ok")
        hot_ok = sem("hot_ok")
        g_ok = sem("g_ok")
        g_used = sem("g_used")
        au_used = sem("au_used")
        m_hi = sem("m_hi")
        m_lo = sem("m_lo")

        block = ctx.enter_context(nc.Block())

        def flat(ap):
            return ap.rearrange("p a b -> p (a b)")

        def sample(ap):
            return ap.rearrange("p c (b s) -> p c b s", b=DEC_B)

        def unit_ap(tensor, k):
            return tensor[:, bass.ds(k, 1), :].rearrange("p o n -> p (o n)")

        @block.sync
        def _(sp):
            quads = stream.rearrange("(q j) p n -> j q p n", j=4)
            for j in range(4):
                sp.dma_start(raw[:, j, :], quads[j, 0]).then_inc(raw_in[j], 16)
            with sp.Fori(1, DEPTH * QUADS) as q:
                free = [sp.snap(q * 4 + (j - 3)) for j in range(4)]
                for j in range(4):
                    src = quads[j][bass.ds(q, 1)].rearrange("o p n -> (o p) n")
                    sp.wait_ge(lo, free[j])
                    sp.dma_start(raw[:, j, :], src).then_inc(raw_in[j], 16)

        @block.gpsimd
        def _(pool):
            pool.dma_start(gains[:, :, :, :], gains_in).then_inc(gains_got, 16)
            pool.dma_start(x[:, :, :], x_in).then_inc(x_got, 16)
            pool.iota(iota[:, :], [[1, P]], base=0, channel_multiplier=0,
                      allow_small_or_imprecise_dtypes=True).then_inc(const_pool, 1)
            pool.wait_ge(const_dve, 3)
            pool.affine_select(ident[:, :], ident[:, :], [[-1, P]], ALU.is_equal, 0.0, base=0,
                               channel_multiplier=1).then_inc(const_pool, 1)
            with pool.Fori(0, DEPTH) as L:
                pool.wait_ge(x_new, L * 3 + 1)
                pool.sem_inc(passed, 1)
                pool.memset(ws_blk[:, :, :], 0.0)
                pool.drain()
                pool.dma_start(ws[:, :, :], ws_in[bass.ds(L, 1)].rearrange("o p g t -> (o p) g t")
                               ).then_inc(mixw_got, 16)
                pool.dma_start(bias[:, :, :], bias_in[bass.ds(L, 1)]).then_inc(mixw_got, 16)
                pool.dma_start(prev[:, :, :, :].rearrange("p c b s -> p (c b s)"),
                               conv_in[bass.ds(L, 1)].rearrange("o p c b s -> (o p) (c b s)")
                               ).then_inc(conv_got, 16)
                for b in range(DEC_B):
                    pool.dma_start(ws_blk[DEC_S * b:DEC_S * b + DEC_S, :, DEC_S * b:DEC_S * b + DEC_S],
                                   ws_blk_in[bass.ds(L, 1)].rearrange("o s g t -> (o s) g t")
                                   ).then_inc(mixw_got, 16)
                pool.wait_ge(mixw_got, L * 160 + 160)
                pool.sem_inc(passed, 1)
                pool.affine_select(ws[:, :, :], ws[:, :, :], [[0, GROUPS], [1, CHUNK]], ALU.is_ge, 0.0,
                                   base=0, channel_multiplier=-1)
                pool.affine_select(ws_blk[:, :, :], ws_blk[:, :, :], [[0, GROUPS], [1, DEC]], ALU.is_ge,
                                   0.0, base=0, channel_multiplier=-1)
                pool.drain().then_inc(mixw_ok, 1)
                pool.wait_ge(nt_ok, L * NORMS + 2)
                pool.sem_inc(passed, 1)
                pool.dma_start(v_out[bass.ds(L, 1)].rearrange("o p c t -> (o p) c t"),
                               t_op[:, :, SEQ:T]).then_inc(out_v, 16)
                pool.wait_ge(cx_ok, L + 1)
                pool.sem_inc(passed, 1)
                pool.dma_start(conv_out[bass.ds(L, 1)].rearrange("o p c s -> (o p) (c s)"),
                               flat(after[:, :, :])).then_inc(out_c, 16)
                pool.wait_ge(s_used, L * GROUPS + GROUPS)
                pool.sem_inc(passed, 1)
                pool.dma_start(keys[:, :, :], keys_in[bass.ds(L, 1)].rearrange("o p h k -> (o p) h k")
                               ).then_inc(keys_got, 16)
                pool.wait_ge(x_new, L * 3 + 2)
                pool.sem_inc(passed, 1)
                pool.dma_start(x_keep, flat(x[:, :, :])).then_inc(kept, 16)
                pool.wait_ge(rT_in, L + 1)
                pool.sem_inc(passed, 1)
                pool.memset(mat[:, E_MIX:KEYS, :], 1.0).then_inc(one_ok, 1)
                pool.wait_ge(m_lo, L * KEYS + KEYS)
                pool.sem_inc(passed, 1)
                pool.dma_start(flat(x[:, :, :]), x_keep).then_inc(back, 16)
                pool.dma_start(z[:, 0:CP, :], pe_in[bass.ds(L, 1)].rearrange("o p c t -> (o p) c t")
                               ).then_inc(pe_got, 16)
            pool.wait_ge(nt_ok, DEPTH * NORMS + 1)
            pool.dma_start(y_out, t_op[:, :, :]).then_inc(out_y, 16)
            pool.wait_ge(out_v, 16 * DEPTH)
            pool.wait_ge(out_c, 16 * DEPTH)
            pool.wait_ge(kept, 16 * DEPTH)
            pool.wait_ge(out_y, 16)

        @block.scalar
        def _(act):
            for _ in range(4):
                act.nop().then_inc(evac, 1)
            act.wait_ge(const_dve, 3)
            act.wait_ge(x_got, 16)
            with act.Fori(0, DEPTH) as L:
                q0 = act.snap(L * QUADS)
                u0 = act.snap(L * UNITS)

                def split(q, j):
                    act.wait_ge(raw_in[j], (q0 + q) * 16 + 16)
                    act.activation(w_hi[:, j % 2, :], raw[:, j, :], ACT.Copy).then_inc(hi, 1)

                def step(q, j, last=False):
                    act.wait_ge(mm, u0 + q * 4 + (j + 1))
                    if not last:
                        split(q + (j + 2) // 4, (j + 2) % 4)

                def segment(q_first, quads, evacuate):
                    with act.Fori(0, quads) as i:
                        for j in range(4):
                            step(i + q_first, j)
                            evacuate(i, j).then_inc(evac, 1)

                def squares(n, src):
                    act.activation(sq, src, ACT.Square).then_inc(sq_ok, 1)

                def mean_root(n):
                    act.wait_ge(ss_ok, L * NORMS + n)
                    act.activation(root[:, :], ps[:, 4, 0:T], ACT.Sqrt, bias=eps[:, 0:1],
                                   scale=1.0 / D).then_inc(rt_ok, 1)

                def upper(dst, src):
                    act.activation(dst, src, ACT.Copy).then_inc(op_hi, 1)

                def to_z(first, func):
                    def evacuate(i, j):
                        return act.activation(unit_ap(z, i * 4 + (first + j)), ps[:, j, 0:T], func)
                    return evacuate

                act.wait_ge(x_new, L * 3 + 1)
                squares(1, x[:, :, :])
                split(0, 0)
                split(0, 1)
                mean_root(1)
                act.wait_ge(nt_ok, L * NORMS + 1)
                upper(h_hi[:, :, :], t_op[:, :, :])
                segment(0, 2, to_z(0, ACT.Gelu_apprx_tanh))
                act.drain()
                squares(2, z[:, 0:C, :])
                segment(2, 2, to_z(8, ACT.Gelu_apprx_tanh))
                mean_root(2)
                segment(4, 2, to_z(16, ACT.Copy))
                for k in range(3):
                    act.wait_ge(tr_ok, L * 3 + (k + 1))
                    for half in range(2):
                        rows = P if k < 2 else DEC
                        a = act.activation(v_tok[0:rows, k, half * 512:half * 512 + 512],
                                           ps[0:rows, 4 + (2 * k + half) % 4, :], ACT.Copy)
                    a.then_inc(tok_ok, 1)
                segment(6, 2, to_z(24, ACT.Copy))
                segment(8, 2, to_z(32, ACT.Copy))
                segment(10, 2, to_z(40, ACT.Sigmoid))
                segment(12, 2, to_z(48, ACT.Sigmoid))
                act.wait_ge(ab_ok, L + 1)
                upper(h_hi[:, :, :], z[:, 8:16, :])
                upper(b_hi[:, :, :], z[:, 32:40, :])
                segment(Q_A, 2, to_z(0, ACT.Copy))
                segment(Q_B, 2, to_z(16, ACT.Copy))
                act.wait_ge(mix_ok, L + 1)
                upper(h_hi[:, :, :], t_op[:, :, :])
                segment(Q_O, 2, to_z(24, ACT.Copy))
                act.wait_ge(x_new, L * 3 + 2)
                squares(3, x[:, :, :])
                mean_root(3)
                act.wait_ge(nt_ok, L * NORMS + 3)
                upper(h_hi[:, :, :], t_op[:, :, :])
                segment(Q_Q, 4, to_z(0, ACT.Copy))
                act.wait_ge(out_c, L * 16 + 16)
                for g in range(ROUTES // 2):
                    act.wait_ge(sc_ok, L * (ROUTES // 2) + (g + 1))
                    act.activation(scores[:, 2 * g:2 * g + 2, :, :].rearrange("p a b k -> p (a b k)"),
                                   ps[0:TT, 4 + g % 4, :], ACT.Copy).then_inc(sc_in, 1)

                def to_mat(i, j):
                    return act.activation(unit_ap(mat, i * 4 + j), ps[:, j, 0:T], ACT.Gelu_apprx_tanh)

                act.wait_ge(kept, L * 16 + 16)
                segment(Q_U, U_TOP, to_mat)
                act.wait_ge(top_ok, L + 1)
                act.activation(route[:, 2, :, :].rearrange("p r k -> p (r k)"),
                               route[:, 2, :, :].rearrange("p r k -> p (r k)"), ACT.Exp).then_inc(ex_ok, 1)

                def to_mat2(i, j):
                    return act.activation(unit_ap(mat, i * 4 + (4 * U_TOP + j)), ps[:, j, 0:T],
                                          ACT.Gelu_apprx_tanh)

                segment(Q_U + U_TOP, U_ONLY, to_mat2)
                with act.Fori(0, U_MIX) as i:
                    for j in range(4):
                        step(i + (Q_U + U_TOP + U_ONLY), j)
                        act.wait_ge(au_used, L * (4 * U_MIX) + i * 4 + (j + 1))
                        act.activation(act_u[:, j % 2, :], ps[:, j, 0:T], ACT.Gelu_apprx_tanh).then_inc(evac, 1)

                def mat_upper(e, j):
                    act.activation(h_hi[:, j, :], unit_ap(mat, e), ACT.Copy).then_inc(m_hi, 1)

                act.wait_ge(au_used, L * (4 * U_MIX) + (4 * U_MIX + 2))
                act.wait_ge(g_used, L * (T // 4) + (T // 4 + 2))
                mat_upper(0, 0)
                mat_upper(1, 1)
                with act.Fori(0, KEYS // 4 - 1) as i:
                    for j in range(4):
                        step(i + Q_V, j)
                        mat_upper(i * 4 + (j + 2), (j + 2) % 4)
                for j in range(4):
                    step(Q_PG - 1, j)
                    if j < 2:
                        mat_upper(KEYS - 2 + j, j + 2)

                act.wait_ge(x_new, L * 3 + 3)
                squares(4, x[:, :, :])
                mean_root(4)
                act.wait_ge(nt_ok, L * NORMS + 4)
                upper(h_hi[:, :, :], t_op[:, :, :])
                act.wait_ge(pe_got, L * 16 + 16)
                upper(b_hi[:, 0:CP, :], z[:, 0:CP, :])
                segment(Q_PG, 2, to_z(8, ACT.Sigmoid))
                for j in range(4):
                    step(Q_PLE, j, last=(j >= 2))
                    for k in range(2):
                        a = act.activation(z[:, 16 + 2 * j + k, :], ps[:, (2 * j + k) % 4, 0:T], ACT.Copy)
                    a.then_inc(evac, 1)
            act.wait_ge(x_new, DEPTH * 3 + 1)
            act.activation(sq, x[:, :, :], ACT.Square).then_inc(sq_ok, 1)
            act.wait_ge(ss_ok, DEPTH * NORMS + 1)
            act.activation(root[:, :], ps[:, 4, 0:T], ACT.Sqrt, bias=eps[:, 0:1], scale=1.0 / D).then_inc(rt_ok, 1)

        @block.vector
        def _(dve):
            dve.memset(ones[:, :], 1.0).then_inc(const_dve, 1)
            dve.memset(ident[:, :], 1.0).then_inc(const_dve, 1)
            dve.memset(eps[:, :], EPS).then_inc(const_dve, 1)
            for _ in range(2):
                dve.nop().then_inc(au_used, 1)
                dve.nop().then_inc(g_used, 1)
            dve.wait_ge(gains_got, 16)
            dve.wait_ge(x_got, 16)
            dve.wait_ge(const_pool, 2)
            dve.nop().then_inc(x_new, 1)

            def norm(gain_of, n, src):
                dve.wait_ge(rt_ok, n)
                dve.reciprocal(root[:, :], root[:, :])
                dve.drain()
                for c in range(C):
                    t = dve.scalar_tensor_tensor(out=t_op[:, c, :], in0=src[:, c, :], scalar=gain_of(c),
                                                 in1=root[:, :], op0=ALU.mult, op1=ALU.mult)
                t.then_inc(nt_ok, 1)
                dve.drain()

            with dve.Fori(0, DEPTH) as L:
                u0 = dve.snap(L * UNITS)

                def split(q, j):
                    dve.wait_ge(hi, u0 + q * 4 + (j + 1))
                    dve.tensor_tensor(w_lo[:, j % 2, :], raw[:, j, :], w_hi[:, j % 2, :].bitcast(F32),
                                      ALU.subtract).then_inc(lo, 1)

                def ahead(q, j):
                    split(q + (j + 2) // 4, (j + 2) % 4)

                def segment(q_first, quads):
                    dve.sem_inc(passed, 1)
                    with dve.Fori(0, quads) as i:
                        for j in range(4):
                            ahead(i + q_first, j)

                def gain(kind):
                    return lambda c: gains[:, bass.ds(L, 1), kind, c:c + 1].rearrange("p o c -> p (o c)")

                def evacuated(quads):
                    dve.wait_ge(evac, L * EVACS + (4 + 4 * quads))

                def lower(n, dst, src, upper_half):
                    dve.wait_ge(op_hi, L * PREPS + n)
                    dve.tensor_tensor(dst, src, upper_half.bitcast(F32), ALU.subtract).then_inc(op_lo, 1)

                split(0, 0)
                split(0, 1)
                norm(gain(0), L * NORMS + 1, x)
                lower(1, h_lo[:, :, :], t_op[:, :, :], h_hi[:, :, :])
                segment(0, 2)
                segment(2, 2)
                norm(gain(1), L * NORMS + 2, z)
                segment(4, 2)
                segment(6, 2)
                for g in range(GROUPS):
                    dve.wait_ge(s_ok, L * GROUPS + (g + 1))
                    dve.tensor_tensor(z[:, 8 + g, :], ps[:, 4 + g % 4, 0:T], z[:, 8 + g, :],
                                      ALU.mult).then_inc(s_used, 1)
                evacuated(8)
                dve.wait_ge(conv_got, L * 16 + 16)
                dve.memset(ext[:, :, 0:2], 0.0)
                dve.tensor_tensor(ext[:, :, 2:2 + SEQ], z[:, 16:24, 0:SEQ], z[:, 24:32, 0:SEQ], ALU.mult)
                dve.tensor_tensor(sample(ext[:, :, 2 + SEQ:EXT])[:, :, :, 2:], sample(z[:, 16:24, SEQ:T]),
                                  sample(z[:, 24:32, SEQ:T]), ALU.mult)
                dve.tensor_copy(sample(ext[:, :, 2 + SEQ:EXT])[:, :, :, 0:2], prev[:, :, :, :])
                dve.drain()
                dve.tensor_copy(after[:, :, 0:2], ext[:, :, SEQ:SEQ + 2])
                dve.tensor_copy(sample(after[:, :, 2:]), sample(ext[:, :, 2 + SEQ:EXT])[:, :, :, DEC_S:]
                                ).then_inc(cx_ok, 1)
                segment(8, 2)
                segment(10, 1)
                N = EXT - 2
                tap = flat(z[:, 16:32, :])[:, 0:C * EXT].rearrange("p (c n) -> p c n", c=C)
                for k in range(3):
                    for c in range(C):
                        w = gain(4 + k)(c)
                        if k == 0:
                            dve.tensor_scalar(tap[:, c, 0:N], ext[:, c, 0:N], w, None, ALU.mult)
                        else:
                            dve.scalar_tensor_tensor(out=tap[:, c, 0:N], in0=ext[:, c, k:k + N], scalar=w,
                                                     in1=tap[:, c, 0:N], op0=ALU.mult, op1=ALU.add)
                    dve.drain()
                evacuated(10)
                dve.tensor_tensor(z[:, 32:40, 0:SEQ], z[:, 32:40, 0:SEQ], tap[:, :, 0:SEQ], ALU.mult)
                dve.tensor_tensor(sample(z[:, 32:40, SEQ:T]), sample(z[:, 32:40, SEQ:T]),
                                  sample(tap[:, :, 2 + SEQ:EXT])[:, :, :, 0:DEC_S], ALU.mult).then_inc(ab_ok, 1)
                dve.drain()
                segment(11, 3)
                lower(2, h_lo[:, :, :], z[:, 8:16, :], h_hi[:, :, :])
                lower(3, b_lo[:, :, :], z[:, 32:40, :], b_hi[:, :, :])
                segment(Q_A, 2)
                evacuated(Q_A + 2)
                dve.tensor_tensor(z[:, 0:8, :], z[:, 0:8, :], z[:, 40:48, :], ALU.mult)
                segment(Q_B, 2)
                evacuated(Q_B + 2)
                dve.tensor_tensor(z[:, 16:24, :], z[:, 16:24, :], z[:, 48:56, :], ALU.mult)
                dve.drain()
                dve.wait_ge(out_v, L * 16 + 16)
                dve.tensor_tensor(t_op[:, :, :], z[:, 0:8, :], z[:, 16:24, :], ALU.add).then_inc(mix_ok, 1)
                lower(4, h_lo[:, :, :], t_op[:, :, :], h_hi[:, :, :])
                segment(Q_O, 2)
                evacuated(Q_O + 2)
                dve.tensor_tensor(x[:, :, :], x[:, :, :], z[:, 24:32, :], ALU.add).then_inc(x_new, 1)
                dve.drain()
                norm(gain(2), L * NORMS + 3, x)
                lower(5, h_lo[:, :, :], t_op[:, :, :], h_hi[:, :, :])
                segment(Q_Q, 4)

                def top16(dst, idx, src, spare):
                    dve.max(dst[:, 0:8], src)
                    dve.drain()
                    dve.max_index(idx[:, 0:8], dst[:, 0:8], src)
                    dve.match_replace(spare, dst[:, 0:8], src, LOWEST)
                    dve.drain()
                    dve.max(dst[:, 8:16], spare)
                    dve.drain()
                    dve.max_index(idx[:, 8:16], dst[:, 8:16], spare)

                def choose(r):
                    dve.tensor_copy(row[:, :, :], scores[:, bass.ds(r, 1), :, :].rearrange("p o h k -> p (o h) k"))
                    dve.drain()
                    for half in range(2):
                        top16(best[:, half, :], besti[:, half, :], row[:, half, :], cut[:, half, :])
                    dve.drain()
                    dve.tensor_copy(bestf[:, :, :], besti[:, :, :])
                    dve.tensor_tensor(cand[:, :, :], best[:, 0, :].unsqueeze(2).to_broadcast([TT, TOPK, TOPK]),
                                      best[:, 1, :].unsqueeze(1).to_broadcast([TT, TOPK, TOPK]), ALU.add)
                    dve.drain()
                    top16(top[:, :], pick[:, :], flat(cand[:, :, :]), flat(cand2[:, :, :]))
                    dve.drain()
                    dve.tensor_scalar(pick2[:, 0, :], pick[:, :], 4, None, ALU.logical_shift_right)
                    dve.tensor_scalar(pick2[:, 1, :], pick[:, :], 15, None, ALU.bitwise_and)
                    dve.drain()
                    dve.tensor_copy(pickf[:, :, :], pick2[:, :, :])
                    dve.drain()
                    for half in range(2):
                        dve.tensor_tensor(hit[:, half, :, :],
                                          pickf[:, half, :].unsqueeze(2).to_broadcast([TT, TOPK, TOPK]),
                                          iota[0:TT, 0:TOPK].unsqueeze(1).to_broadcast([TT, TOPK, TOPK]), ALU.is_equal)
                    dve.drain()
                    for half in range(2):
                        dve.tensor_tensor(hit[:, half, :, :], hit[:, half, :, :],
                                          bestf[:, half, :].unsqueeze(1).to_broadcast([TT, TOPK, TOPK]), ALU.mult)
                    dve.drain()
                    dve.tensor_reduce(route[:, 0:2, bass.ds(r, 1), :].rearrange("p h o k -> p h (o k)"),
                                      hit[:, :, :, :], AX.X, ALU.add)
                    dve.tensor_scalar(route[:, 2, bass.ds(r, 1), :].rearrange("p o k -> p (o k)"), top[:, :],
                                      top[:, 0:1], None, ALU.subtract)

                dve.wait_ge(sc_in, L * (ROUTES // 2) + ROUTES // 2)
                dve.sem_inc(passed, 1)
                with dve.Fori(0, U_TOP) as i:
                    for j in range(4):
                        ahead(i + Q_U, j)
                        if j % 2 == 1:
                            choose(i * 2 + j // 2)
                dve.drain().then_inc(top_ok, 1)
                segment(Q_U + U_TOP, 1)
                dve.wait_ge(ex_ok, L + 1)
                dve.tensor_reduce(total[:, :], route[:, 2, :, :], AX.X, ALU.add)
                dve.drain()
                dve.reciprocal(total[:, :], total[:, :])
                dve.drain()
                dve.tensor_tensor(route[:, 2, :, :], route[:, 2, :, :],
                                  total[:, :].unsqueeze(2).to_broadcast([TT, ROUTES, TOPK]), ALU.mult)
                dve.drain().then_inc(rt_w, 1)
                segment(Q_U + U_TOP + 1, U_ONLY - 1)
                dve.wait_ge(rT_ok, L + 1)
                for k in range(3):
                    dve.tensor_copy(routeT[:, k, :], ps[:, 4 + k, 0:T])
                dve.drain().then_inc(rT_in, 1)

                def one_hots(g):
                    for k in range(4):
                        def col(a):
                            return routeT[:, a, bass.ds(g * 4 + k, 1)]
                        dve.tensor_scalar(hot1[:, k, :], iota[:, :], col(0), col(2), ALU.is_equal, ALU.mult)
                        dve.tensor_scalar(hot2[:, k, :], iota[:, :], col(1), None, ALU.is_equal)
                    dve.drain().then_inc(hot_ok, 1)

                dve.wait_ge(one_ok, L + 1)
                dve.sem_inc(passed, 1)
                with dve.Fori(0, U_MIX) as i:
                    for j in range(4):
                        g = i * 4 + j
                        one_hots(g)
                        ahead(i + (Q_U + U_TOP + U_ONLY), j)
                        dve.wait_ge(evac, L * EVACS + g + (4 * (Q_U + U_TOP + U_ONLY) + 5))
                        tile = unit_ap(mat, i * 4 + (E_MIX + j))
                        dve.tensor_tensor(tile, tile, act_u[:, j % 2, :], ALU.mult).then_inc(au_used, 1)
                        dve.drain()
                        dve.wait_ge(g_ok, L * (T // 4) + g + 1)
                        part = mat[:, :, bass.ds(g * 4, 4)]
                        dve.tensor_tensor(part, part, ps[:, 4 + j % 2, :].rearrange("p (k e) -> p e k", k=4),
                                          ALU.mult).then_inc(g_used, 1)
                        dve.drain()

                def mat_lower(e, j):
                    dve.wait_ge(m_hi, L * KEYS + e + 1)
                    dve.tensor_tensor(h_lo[:, j, :], unit_ap(mat, e), h_hi[:, j, :].bitcast(F32),
                                      ALU.subtract).then_inc(m_lo, 1)

                mat_lower(0, 0)
                mat_lower(1, 1)
                with dve.Fori(0, KEYS // 4 - 1) as i:
                    for j in range(4):
                        ahead(i + Q_V, j)
                        mat_lower(i * 4 + (j + 2), (j + 2) % 4)
                for j in range(4):
                    ahead(Q_PG - 1, j)
                    if j < 2:
                        mat_lower(KEYS - 2 + j, j + 2)
                dve.wait_ge(mm, u0 + 4 * Q_PG)
                dve.wait_ge(back, L * 16 + 16)
                for c in range(C):
                    dve.tensor_tensor(x[:, c, :], x[:, c, :], ps[:, c, 0:T], ALU.add)
                dve.drain().then_inc(x_new, 1)
                norm(gain(3), L * NORMS + 4, x)
                lower(6, h_lo[:, :, :], t_op[:, :, :], h_hi[:, :, :])
                lower(7, b_lo[:, 0:CP, :], z[:, 0:CP, :], b_hi[:, 0:CP, :])
                segment(Q_PG, 2)
                for j in range(2):
                    ahead(Q_PLE, j)
                evacuated(QUADS - KEYS // 4)
                dve.tensor_tensor(z[:, 16:24, :], z[:, 16:24, :], z[:, 8:16, :], ALU.mult)
                dve.drain()
                dve.tensor_tensor(x[:, :, :], x[:, :, :], z[:, 16:24, :], ALU.add).then_inc(x_new, 1)
                dve.drain()
            norm(lambda c: gains[:, 0, 7, c:c + 1], DEPTH * NORMS + 1, x)

        @block.tensor
        def _(pe):
            pe.wait_ge(const_dve, 3)
            pe.wait_ge(const_pool, 2)

            def sum_squares(n):
                pe.wait_ge(sq_ok, n)
                for c in range(C):
                    m = pe.matmul(ps[:, 4, 0:T], ones[:, :], sq[:, c, :], start=(c == 0), stop=(c == C - 1))
                m.then_inc(ss_ok, 1)

            with pe.Fori(0, DEPTH) as L:
                u0 = pe.snap(L * UNITS)
                e0 = pe.snap(L * EVACS)

                def product(out, w, j, col, rhs_hi, rhs_lo, first, last):
                    wh = w_hi[:, j % 2, col:col + P]
                    wl = w_lo[:, j % 2, col:col + P]
                    pe.matmul(out, wh, rhs_hi, start=first, stop=False)
                    pe.matmul(out, wh, rhs_lo, start=False, stop=False)
                    return pe.matmul(out, wl, rhs_hi, start=False, stop=last)

                def unit(q, j, evac_q, a_hi, a_lo):
                    pe.wait_ge(lo, u0 + q * 4 + (j + 1))
                    pe.wait_ge(evac, e0 + evac_q * 4 + (j + 1))
                    for c in range(C):
                        m = product(ps[:, j, 0:T], None, j, c * P, a_hi[:, c, :], a_lo[:, c, :], c == 0, c == C - 1)
                    m.then_inc(mm, 1)

                def segment(q_first, quads, a_hi=h_hi, a_lo=h_lo, skipped=0):
                    pe.sem_inc(passed, 1)
                    with pe.Fori(0, quads) as i:
                        for j in range(4):
                            unit(i + q_first, j, i + (q_first - skipped), a_hi, a_lo)

                def operand(n):
                    pe.wait_ge(op_lo, L * PREPS + n)

                sum_squares(L * NORMS + 1)
                operand(1)
                segment(0, 4)
                sum_squares(L * NORMS + 2)
                segment(4, 2)
                pe.wait_ge(nt_ok, L * NORMS + 2)
                for k in range(3):
                    n = P if k < 2 else DEC
                    if k == 2:
                        pe.wait_ge(tok_ok, L * 3 + 1)
                    for c in range(C):
                        m = pe.transpose(ps[0:n, 4 + (2 * k + c // 4) % 4, c % 4 * P:c % 4 * P + P],
                                         t_op[:, c, k * P:k * P + n], ident[:, :])
                    m.then_inc(tr_ok, 1)
                segment(6, 2)
                pe.wait_ge(tok_ok, L * 3 + 3)
                pe.wait_ge(mixw_ok, L + 1)
                for g in range(GROUPS):
                    if g >= 4:
                        pe.wait_ge(s_used, L * GROUPS + (g - 3))
                    out = ps[:, 4 + g % 4, 0:T]
                    pe.matmul(out, ones[0:1, :], bias[0:1, g, :], start=True, stop=False)
                    for k in range(2):
                        pe.matmul(out[:, k * P:k * P + P], v_tok[:, k, g * P:g * P + P], ws[:, g, :],
                                  start=False, stop=False)
                    pe.matmul(out[:, SEQ:T], v_tok[0:DEC, 2, g * P:g * P + P], ws_blk[:, g, :],
                              start=False, stop=True).then_inc(s_ok, 1)
                segment(8, 6)
                operand(2)
                segment(Q_A, 2)
                operand(3)
                segment(Q_B, 2, b_hi, b_lo)
                operand(4)
                segment(Q_O, 2)
                sum_squares(L * NORMS + 3)
                operand(5)
                segment(Q_Q, 4)
                pe.wait_ge(keys_got, L * 16 + 16)
                pe.wait_ge(evac, e0 + (4 + 4 * (Q_Q + 4)))
                for r in range(ROUTES):
                    g, tile, head = r // 2, r // HEADS, r % HEADS
                    if r % 2 == 0 and g >= 4:
                        pe.wait_ge(sc_in, L * (ROUTES // 2) + (g - 3))
                    for half in range(2):
                        at = r % 2 * 2 * KEYS + half * KEYS
                        m = pe.matmul(ps[0:TT, 4 + g % 4, at:at + KEYS],
                                      z[:, 2 * head + half, tile * TT:tile * TT + TT], keys[:, half, :],
                                      start=True, stop=True)
                    if r % 2:
                        m.then_inc(sc_ok, 1)
                segment(Q_U, U_TOP + U_ONLY)
                pe.wait_ge(rt_w, L + 1)
                for k in range(3):
                    for tile in range(NT):
                        m = pe.transpose(ps[:, 4 + k, tile * TT:tile * TT + TT],
                                         route[:, k, tile * HEADS:tile * HEADS + HEADS, :].rearrange(
                                             "p r k -> p (r k)"), ident[0:TT, 0:TT])
                m.then_inc(rT_ok, 1)
                with pe.Fori(0, U_MIX) as i:
                    for j in range(4):
                        q = i + (Q_U + U_TOP + U_ONLY)
                        unit(q, j, q, h_hi, h_lo)
                        pe.wait_ge(hot_ok, L * (T // 4) + i * 4 + (j + 1))
                        pe.wait_ge(g_used, L * (T // 4) + i * 4 + (j + 1))
                        for k in range(4):
                            m = pe.matmul(ps[:, 4 + j % 2, k * P:k * P + P], hot2[:, k, :], hot1[:, k, :],
                                          start=True, stop=True)
                        m.then_inc(g_ok, 1)

                def expert_unit(q, j, e, first=False, last=False):
                    pe.wait_ge(lo, u0 + q * 4 + (j + 1))
                    pe.wait_ge(m_lo, L * KEYS + e + 1)
                    for c in range(C):
                        m = product(ps[:, c, 0:T], None, j, c * P, h_hi[:, j, :], h_lo[:, j, :], first, last)
                    m.then_inc(mm, 1)

                for j in range(4):
                    expert_unit(Q_V, j, j, first=(j == 0))
                with pe.Fori(1, KEYS // 4 - 1) as i:
                    for j in range(4):
                        expert_unit(i + Q_V, j, i * 4 + j)
                for j in range(4):
                    expert_unit(Q_PG - 1, j, KEYS - 4 + j, last=(j == 3))

                sum_squares(L * NORMS + 4)
                operand(6)
                segment(Q_PG, 2, skipped=KEYS // 4)
                operand(7)
                for j in range(4):
                    pe.wait_ge(lo, u0 + (4 * Q_PLE + j + 1))
                    pe.wait_ge(evac, e0 + (4 * (Q_PLE - KEYS // 4) + j + 3))
                    for k in range(2):
                        for c in range(CP):
                            m = product(ps[:, (2 * j + k) % 4, 0:T], None, j, (k * CP + c) * P,
                                        b_hi[:, c, :], b_lo[:, c, :], c == 0, c == CP - 1)
                    m.then_inc(mm, 1)
            sum_squares(DEPTH * NORMS + 1)


def kernel(x_prompt, x_sample, state_conv, p_prompt, p_sample, ln1, w_in, ln_v, w_s, b_s, conv_w, w_a, w_b,
           w_o, ln2, w_q, k1, k2, u_tab, v_tab, ln3, w_pg, w_ple, ln_f):
    import numpy as np
    import concourse.bacc as bacc
    from concourse.bass_utils import run_bass_kernel_spmd

    def lay(a):
        return np.ascontiguousarray(np.asarray(a))

    def tiles(w):
        w = np.asarray(w)
        k, n = w.shape
        return w.reshape(k // P, P, n // P, P).transpose(2, 1, 0, 3).reshape(n // P, P, k)

    at = {n: i * 1024 for i, n in enumerate(["u", "v", "b", "c", "x", "ga", "gb"])}
    stream = np.empty((DEPTH * UNITS, P, D), np.float32)
    for l in range(DEPTH):
        parts = []
        wi = np.asarray(w_in[l])
        for n in SEGS:
            parts.append(tiles(wi[:, at[n]:at[n] + 1024]))
        for w in (w_a, w_b, w_o, w_q):
            parts.append(tiles(w[l]))
        parts.append(tiles(np.asarray(u_tab[l]).T))
        parts.append(np.asarray(v_tab[l]).reshape(KEYS, P, D))
        parts.append(tiles(w_pg[l]))
        ple = np.zeros((4, P, D), np.float32)
        ple[:, :, 0:D // 2] = tiles(w_ple[l]).reshape(4, 2, P, CP * P).transpose(0, 2, 1, 3).reshape(4, P, D // 2)
        parts.append(ple)
        k = l * UNITS
        for p in parts:
            stream[k:k + len(p)] = p
            k += len(p)
        assert k == (l + 1) * UNITS

    def tokens(prompt, sample):
        f = prompt.shape[-1]
        a = np.concatenate([np.asarray(prompt).reshape(SEQ, f), np.asarray(sample).reshape(DEC, f)])
        return lay(a.T.reshape(f // P, P, T).transpose(1, 0, 2))

    def per_feature(a):
        return np.asarray(a).reshape(C, P).T

    gains = np.empty((P, DEPTH, 8, C), np.float32)
    for l in range(DEPTH):
        for n, g in enumerate((ln1[l], ln_v[l], ln2[l], ln3[l], conv_w[l, 0], conv_w[l, 1], conv_w[l, 2], ln_f)):
            gains[:, l, n, :] = per_feature(g)
    wsT = np.asarray(w_s).transpose(0, 3, 1, 2)
    bs = np.asarray(b_s)
    bias = np.concatenate([bs, bs] + [bs[:, :, 0:DEC_S]] * DEC_B, axis=2)
    keys = np.stack([np.asarray(k1).transpose(0, 2, 1), np.asarray(k2).transpose(0, 2, 1)], axis=2)
    conv = np.asarray(state_conv).reshape(DEPTH, DEC_B, 2, C, P).transpose(0, 4, 3, 1, 2)
    arrays = {
        "stream": stream,
        "x_in": tokens(x_prompt, x_sample),
        "pe_in": lay(np.stack([tokens(p_prompt[l], p_sample[l]) for l in range(DEPTH)])),
        "conv_in": lay(conv),
        "gains_in": gains,
        "ws_in": lay(wsT),
        "ws_blk_in": lay(wsT[:, 0:DEC_S, :, 0:DEC_S]),
        "bias_in": lay(bias),
        "keys_in": lay(keys),
    }
    nc = bacc.Bacc("TRN2", target_bir_lowering=False, num_devices=1)
    ins = [nc.dram_tensor(n, a.shape, F32, kind="ExternalInput").ap() for n, a in arrays.items()]
    shapes = {"y_out": (P, C, T), "conv_out": (DEPTH, P, C, 2 + 2 * DEC_B),
              "v_out": (DEPTH, P, C, DEC)}
    outs = [nc.dram_tensor(n, sh, F32, kind="ExternalOutput").ap() for n, sh in shapes.items()]
    hybrid_trunk(nc, *ins, *outs)
    got = run_bass_kernel_spmd(nc, [arrays], core_ids=[0]).results[0]
    y = got["y_out"].transpose(2, 1, 0).reshape(T, D)
    after = got["conv_out"]
    cp = after[:, :, :, 0:2].transpose(0, 3, 2, 1).reshape(DEPTH, 1, 2, D)
    cs = after[:, :, :, 2:].reshape(DEPTH, P, C, DEC_B, 2).transpose(0, 3, 4, 2, 1).reshape(DEPTH, DEC_B, 2, D)
    v = got["v_out"].transpose(0, 3, 2, 1).reshape(DEPTH, DEC_B, DEC_S, D)
    return (lay(y[0:SEQ].reshape(1, SEQ, D)), lay(y[SEQ:].reshape(DEC_B, DEC_S, D)), lay(cp), lay(cs), lay(v))
```

```python
import concourse.bass as bass
from concourse import mybir
from contextlib import ExitStack

P = 128
DEPTH = 2
D = 1024
C = D // P
SEQ, DEC_B, DEC_S = 256, 8, 4
DEC = DEC_B * DEC_S
T = SEQ + DEC
CHUNK = 128
GROUPS = 8
HEADS = 8
KEYS = 128
TOPK = 16
D_PLE = 256
CP = D_PLE // P
EPS = 1e-6
TT = 96
NT = T // TT
ROUTES = NT * HEADS
EXT = 2 + SEQ + DEC_B * (2 + DEC_S)

SEGS = ["v", "u", "c", "x", "b", "ga", "gb"]
Q_IN = 0
Q_A = 14
Q_B = 16
Q_O = 18
Q_Q = 20
Q_U = 24
Q_V = Q_U + KEYS // 4
Q_PG = Q_V + KEYS // 4
Q_PLE = Q_PG + 2
QUADS = Q_PLE + 1
UNITS = 4 * QUADS
U_MIX = 12
GROUP = 4
N_GROUPS = T // GROUP
PER_QUAD = N_GROUPS // U_MIX
U_ONLY = 3
U_TOP = KEYS // 4 - U_ONLY - U_MIX
N_FINE = 4 * (U_TOP + U_ONLY)
E_MIX = 4 * (U_TOP + U_ONLY)
EVACS = UNITS - KEYS
NORMS = 4
PREPS = 7

F32 = mybir.dt.float32
F32R = mybir.dt.float32r
U32 = mybir.dt.uint32
ALU = mybir.AluOpType
ACT = mybir.ActivationFunctionType
AX = mybir.AxisListType
LOWEST = -3.0e38


def hybrid_trunk(nc, stream, x_in, pe_in, conv_in, gains_in, ws_in, ws_blk_in, bias_in, keys_in,
                 y_out, conv_out, v_out):
    ctx = ExitStack()
    with ctx:
        def sb(name, shape, dt, where=ctx):
            return where.enter_context(nc.sbuf_tensor(name, shape, dt))

        def sem(name):
            return ctx.enter_context(nc.semaphore(name))

        raw = sb("raw", [P, 4, D], F32)
        w_hi = sb("w_hi", [P, 2, D], F32R)
        w_lo = sb("w_lo", [P, 2, D], F32R)
        h_hi = sb("h_hi", [P, C, T], F32R)
        h_lo = sb("h_lo", [P, C, T], F32R)
        gains = sb("gains", [P, DEPTH, 8, C], F32)
        iota = sb("iota", [P, P], F32)
        ident = sb("ident", [P, P], F32)
        ones = sb("ones", [P, P], F32)
        eps = sb("eps", [P, 1], F32)
        routeT = sb("routeT", [P, 3, T], F32)
        hot1 = sb("hot1", [P, 4, P], F32)
        hot2 = sb("hot2", [P, 4, P], F32)
        act_u = sb("act_u", [P, 2, T], F32)

        front = ExitStack()
        x = sb("x", [P, C, T], F32, front)
        z = sb("z", [P, 7 * C, T], F32, front)
        t_op = sb("t_op", [P, C, T], F32, front)
        b_hi = sb("b_hi", [P, C, T], F32R, front)
        b_lo = sb("b_lo", [P, C, T], F32R, front)
        ext = sb("ext", [P, C, EXT], F32, front)
        root = sb("root", [P, T], F32, front)
        mixer = ExitStack()
        v_tok = sb("v_tok", [P, 3, D], F32, mixer)
        ws = sb("ws", [P, GROUPS, CHUNK], F32, mixer)
        ws_blk = sb("ws_blk", [DEC, GROUPS, DEC], F32, mixer)
        bias = sb("bias", [1, GROUPS, T], F32, mixer)
        prev = sb("prev", [P, C, DEC_B, 2], F32, mixer)
        after = sb("after", [P, C, 2 + 2 * DEC_B], F32, mixer)
        mixer.close()
        routing = ExitStack()
        scores = sb("scores", [TT, ROUTES, 2, KEYS], F32, routing)
        row = sb("row", [TT, 4, KEYS], F32, routing)
        best = sb("best", [TT, 4, TOPK], F32, routing)
        besti = sb("besti", [TT, 4, TOPK], U32, routing)
        bestf = sb("bestf", [TT, 4, TOPK], F32, routing)
        hit = sb("hit", [TT, 4, TOPK, TOPK], F32, routing)
        top = sb("top", [TT, 2, TOPK], F32, routing)
        pick = sb("pick", [TT, 2, TOPK], U32, routing)
        pick2 = sb("pick2", [TT, 4, TOPK], U32, routing)
        pickf = sb("pickf", [TT, 4, TOPK], F32, routing)
        route = sb("route", [TT, 3, ROUTES, TOPK], F32, routing)
        total = sb("total", [TT, ROUTES], F32, routing)
        routing.close()
        front.close()
        mat = sb("mat", [P, KEYS, T], F32)
        sq = ext[:, :, 0:T]
        keys = z[:, 5 * C, 0:2 * KEYS].rearrange("p (h k) -> p h k", h=2)
        cut = hit[:, 0:2, :, :].rearrange("p r (h a) b -> p (r h) (a b)", h=2)
        cand = hit[:, 2:4, :, :]
        cand2 = row[:, :, :].rearrange("p (r h) (a b) -> p r (h a) b", r=2, b=TOPK)

        ps = ctx.enter_context(nc.psum_tensor("ps", [P, 8, 512], F32))
        x_keep = nc.dram_tensor("x_keep", (P, C * T), F32, kind="Internal").ap()

        raw_in = [sem(f"raw_in{j}") for j in range(4)]
        hi = sem("hi")
        lo = sem("lo")
        mm = sem("mm")
        mm_half = sem("mm_half")
        hi_half = sem("hi_half")
        lo_half = sem("lo_half")
        evac = sem("evac")
        passed = sem("passed")
        const_dve = sem("const_dve")
        const_pool = sem("const_pool")
        gains_got = sem("gains_got")
        x_got = sem("x_got")
        conv_got = sem("conv_got")
        mixw_got = sem("mixw_got")
        mixw_ok = sem("mixw_ok")
        pe_got = sem("pe_got")
        keys_got = sem("keys_got")
        kept = sem("kept")
        back = sem("back")
        out_v = sem("out_v")
        out_c = sem("out_c")
        out_y = sem("out_y")
        sq_ok = sem("sq_ok")
        ss_ok = sem("ss_ok")
        rt_ok = sem("rt_ok")
        nt_ok = sem("nt_ok")
        ab_ok = sem("ab_ok")
        mix_ok = sem("mix_ok")
        op_hi = sem("op_hi")
        op_lo = sem("op_lo")
        tr_ok = sem("tr_ok")
        tok_ok = sem("tok_ok")
        s_ok = sem("s_ok")
        s_used = sem("s_used")
        x_new = sem("x_new")
        cx_ok = sem("cx_ok")
        sc_ok = sem("sc_ok")
        sc_in = sem("sc_in")
        top_ok = sem("top_ok")
        ex_ok = sem("ex_ok")
        rt_w = sem("rt_w")
        rT_ok = sem("rT_ok")
        rT_in = sem("rT_in")
        hot_ok = sem("hot_ok")
        g_ok = sem("g_ok")
        g_used = sem("g_used")
        au_used = sem("au_used")
        m_hi = sem("m_hi")
        m_lo = sem("m_lo")

        block = ctx.enter_context(nc.Block())

        def flat(ap):
            return ap.rearrange("p a b -> p (a b)")

        def sample(ap):
            return ap.rearrange("p c (b s) -> p c b s", b=DEC_B)

        def unit_ap(tensor, k):
            return tensor[:, bass.ds(k, 1), :].rearrange("p o n -> p (o n)")

        @block.sync
        def _(sp):
            quads = stream.rearrange("(q j) p n -> j q p n", j=4)
            for j in range(4):
                sp.dma_start(raw[:, j, :], quads[j, 0]).then_inc(raw_in[j], 16)
            with sp.Fori(1, DEPTH * QUADS) as q:
                free = [sp.snap(q * 4 + (j - 3)) for j in range(4)]
                for j in range(4):
                    src = quads[j][bass.ds(q, 1)].rearrange("o p n -> (o p) n")
                    sp.wait_ge(lo, free[j])
                    sp.dma_start(raw[:, j, :], src).then_inc(raw_in[j], 16)

        @block.gpsimd
        def _(pool):
            pool.dma_start(gains[:, :, :, :], gains_in).then_inc(gains_got, 16)
            pool.dma_start(x[:, :, :], x_in).then_inc(x_got, 16)
            pool.iota(iota[:, :], [[1, P]], base=0, channel_multiplier=0,
                      allow_small_or_imprecise_dtypes=True).then_inc(const_pool, 1)
            pool.wait_ge(const_dve, 3)
            pool.affine_select(ident[:, :], ident[:, :], [[-1, P]], ALU.is_equal, 0.0, base=0,
                               channel_multiplier=1).then_inc(const_pool, 1)
            with pool.Fori(0, DEPTH) as L:
                pool.wait_ge(x_new, L * 3 + 1)
                pool.sem_inc(passed, 1)
                pool.memset(ws_blk[:, :, :], 0.0)
                pool.drain()
                pool.dma_start(ws[:, :, :], ws_in[bass.ds(L, 1)].rearrange("o p g t -> (o p) g t")
                               ).then_inc(mixw_got, 16)
                pool.dma_start(bias[:, :, :], bias_in[bass.ds(L, 1)]).then_inc(mixw_got, 16)
                pool.dma_start(prev[:, :, :, :].rearrange("p c b s -> p (c b s)"),
                               conv_in[bass.ds(L, 1)].rearrange("o p c b s -> (o p) (c b s)")
                               ).then_inc(conv_got, 16)
                for b in range(DEC_B):
                    pool.dma_start(ws_blk[DEC_S * b:DEC_S * b + DEC_S, :, DEC_S * b:DEC_S * b + DEC_S],
                                   ws_blk_in[bass.ds(L, 1)].rearrange("o s g t -> (o s) g t")
                                   ).then_inc(mixw_got, 16)
                pool.wait_ge(mixw_got, L * 160 + 160)
                pool.sem_inc(passed, 1)
                pool.affine_select(ws[:, :, :], ws[:, :, :], [[0, GROUPS], [1, CHUNK]], ALU.is_ge, 0.0,
                                   base=0, channel_multiplier=-1)
                pool.affine_select(ws_blk[:, :, :], ws_blk[:, :, :], [[0, GROUPS], [1, DEC]], ALU.is_ge,
                                   0.0, base=0, channel_multiplier=-1)
                pool.drain().then_inc(mixw_ok, 1)
                pool.wait_ge(nt_ok, L * NORMS + 2)
                pool.sem_inc(passed, 1)
                pool.dma_start(v_out[bass.ds(L, 1)].rearrange("o p c t -> (o p) c t"),
                               t_op[:, :, SEQ:T]).then_inc(out_v, 16)
                pool.wait_ge(cx_ok, L + 1)
                pool.sem_inc(passed, 1)
                pool.dma_start(conv_out[bass.ds(L, 1)].rearrange("o p c s -> (o p) (c s)"),
                               flat(after[:, :, :])).then_inc(out_c, 16)
                pool.wait_ge(mix_ok, L + 1)
                pool.sem_inc(passed, 1)
                pool.dma_start(keys[:, :, :], keys_in[bass.ds(L, 1)].rearrange("o p h k -> (o p) h k")
                               ).then_inc(keys_got, 16)
                pool.wait_ge(x_new, L * 3 + 2)
                pool.sem_inc(passed, 1)
                pool.dma_start(x_keep, flat(x[:, :, :])).then_inc(kept, 16)
                pool.wait_ge(lo, L * UNITS + 4 * Q_U + 2)
                pool.sem_inc(passed, 1)
                pool.sem_inc(lo_half, 2)

                def lower(k, lo_col, hi_col):
                    return pool.tensor_tensor(w_lo[:, k % 2, lo_col:hi_col], raw[:, k, lo_col:hi_col],
                                              w_hi[:, k % 2, lo_col:hi_col].bitcast(F32), ALU.subtract)

                with pool.Fori(0, U_TOP + U_ONLY) as i:
                    for j in range(4):
                        pool.wait_ge(hi_half, L * N_FINE + i * 4 + (j + 1))
                        lower((j + 2) % 4, 0, D // 2).then_inc(lo_half, 1)
                        pool.wait_ge(hi, L * UNITS + i * 4 + (4 * Q_U + j + 3))
                        lower((j + 2) % 4, D // 2, D).then_inc(lo, 1)
                with pool.Fori(Q_V - U_MIX, Q_V) as q:
                    for j in range(4):
                        pool.wait_ge(hi, L * UNITS + q * 4 + (j + 3))
                        lower((j + 2) % 4, 0, D).then_inc(lo, 1)
                pool.wait_ge(m_lo, L * KEYS + KEYS)
                pool.sem_inc(passed, 1)
                pool.dma_start(flat(x[:, :, :]), x_keep).then_inc(back, 16)
                pool.dma_start(z[:, 0:CP, :], pe_in[bass.ds(L, 1)].rearrange("o p c t -> (o p) c t")
                               ).then_inc(pe_got, 16)
            pool.wait_ge(nt_ok, DEPTH * NORMS + 1)
            pool.dma_start(y_out, t_op[:, :, :]).then_inc(out_y, 16)
            pool.wait_ge(out_v, 16 * DEPTH)
            pool.wait_ge(out_c, 16 * DEPTH)
            pool.wait_ge(kept, 16 * DEPTH)
            pool.wait_ge(out_y, 16)

        @block.scalar
        def _(act):
            for _ in range(4):
                act.nop().then_inc(evac, 1)
            act.wait_ge(const_dve, 3)
            act.wait_ge(x_got, 16)
            with act.Fori(0, DEPTH) as L:
                q0 = act.snap(L * QUADS)
                u0 = act.snap(L * UNITS)

                def split(q, j):
                    act.wait_ge(raw_in[j], (q0 + q) * 16 + 16)
                    act.activation(w_hi[:, j % 2, :], raw[:, j, :], ACT.Copy).then_inc(hi, 1)

                def step(q, j, last=False):
                    act.wait_ge(mm, u0 + q * 4 + (j + 1))
                    if not last:
                        split(q + (j + 2) // 4, (j + 2) % 4)

                def segment(q_first, quads, evacuate):
                    with act.Fori(0, quads) as i:
                        for j in range(4):
                            act.wait_ge(mm, u0 + i * 4 + (4 * q_first + j + 1))
                            evacuate(i, j).then_inc(evac, 1)
                            split(i + (q_first + (j + 2) // 4), (j + 2) % 4)

                def fine_segment(first, quads):
                    with act.Fori(first, first + quads) as i:
                        for j in range(4):
                            k = (j + 2) % 4
                            act.wait_ge(mm_half, L * N_FINE + i * 4 + (j + 1))
                            act.wait_ge(raw_in[k], (q0 + i) * 16 + (16 * (Q_U + (j + 2) // 4) + 16))
                            act.activation(w_hi[:, k % 2, 0:D // 2], raw[:, k, 0:D // 2], ACT.Copy
                                           ).then_inc(hi_half, 1)
                            act.wait_ge(mm, u0 + i * 4 + (4 * Q_U + j + 1))
                            act.activation(w_hi[:, k % 2, D // 2:D], raw[:, k, D // 2:D], ACT.Copy
                                           ).then_inc(hi, 1)
                            act.activation(unit_ap(mat, i * 4 + j), ps[:, j, 0:T], ACT.Gelu_apprx_tanh
                                           ).then_inc(evac, 1)

                def squares(n, src):
                    act.activation(sq, src, ACT.Square).then_inc(sq_ok, 1)

                def mean_root(n):
                    act.wait_ge(ss_ok, L * NORMS + n)
                    act.activation(root[:, :], ps[:, 4, 0:T], ACT.Sqrt, bias=eps[:, 0:1],
                                   scale=1.0 / D).then_inc(rt_ok, 1)

                def upper(dst, src):
                    act.activation(dst, src, ACT.Copy).then_inc(op_hi, 1)

                def to_z(first, func):
                    def evacuate(i, j):
                        return act.activation(unit_ap(z, i * 4 + (first + j)), ps[:, j, 0:T], func)
                    return evacuate

                act.wait_ge(x_new, L * 3 + 1)
                squares(1, x[:, :, :])
                split(0, 0)
                split(0, 1)
                mean_root(1)
                act.wait_ge(nt_ok, L * NORMS + 1)
                upper(h_hi[:, :, :], t_op[:, :, :])
                segment(0, 2, to_z(0, ACT.Gelu_apprx_tanh))
                act.drain()
                squares(2, z[:, 0:C, :])
                segment(2, 2, to_z(8, ACT.Gelu_apprx_tanh))
                mean_root(2)
                segment(4, 2, to_z(16, ACT.Copy))
                for k in range(3):
                    act.wait_ge(tr_ok, L * 3 + (k + 1))
                    for half in range(2):
                        rows = P if k < 2 else DEC
                        a = act.activation(v_tok[0:rows, k, half * 512:half * 512 + 512],
                                           ps[0:rows, 4 + (2 * k + half) % 4, :], ACT.Copy)
                    a.then_inc(tok_ok, 1)
                segment(6, 2, to_z(24, ACT.Copy))
                segment(8, 2, to_z(32, ACT.Copy))
                segment(10, 2, to_z(40, ACT.Sigmoid))
                segment(12, 2, to_z(48, ACT.Sigmoid))
                act.wait_ge(ab_ok, L + 1)
                upper(h_hi[:, :, :], z[:, 8:16, :])
                upper(b_hi[:, :, :], z[:, 32:40, :])
                segment(Q_A, 2, to_z(0, ACT.Copy))
                segment(Q_B, 2, to_z(16, ACT.Copy))
                act.wait_ge(mix_ok, L + 1)
                upper(h_hi[:, :, :], t_op[:, :, :])
                segment(Q_O, 2, to_z(24, ACT.Copy))
                act.wait_ge(x_new, L * 3 + 2)
                squares(3, x[:, :, :])
                mean_root(3)
                act.wait_ge(nt_ok, L * NORMS + 3)
                upper(h_hi[:, :, :], t_op[:, :, :])
                segment(Q_Q, 4, to_z(0, ACT.Copy))
                act.wait_ge(out_c, L * 16 + 16)
                for g in range(ROUTES // 2):
                    act.wait_ge(sc_ok, L * (ROUTES // 2) + (g + 1))
                    act.activation(scores[:, 2 * g:2 * g + 2, :, :].rearrange("p a b k -> p (a b k)"),
                                   ps[0:TT, 4 + g % 4, :], ACT.Copy).then_inc(sc_in, 1)

                act.wait_ge(kept, L * 16 + 16)
                act.activation(act_u[:, 0, 0:1], eps[:, :], ACT.Gelu_apprx_tanh)
                fine_segment(0, U_TOP)
                act.wait_ge(top_ok, L + 1)
                act.activation(route[:, 2, :, :], route[:, 2, :, :], ACT.Exp).then_inc(ex_ok, 1)

                act.activation(act_u[:, 0, 0:1], eps[:, :], ACT.Gelu_apprx_tanh)
                fine_segment(U_TOP, U_ONLY)
                with act.Fori(0, U_MIX) as i:
                    for j in range(4):
                        step(i + (Q_U + U_TOP + U_ONLY), j)
                        act.wait_ge(au_used, L * (4 * U_MIX) + i * 4 + (j + 1))
                        act.activation(act_u[:, j % 2, :], ps[:, j, 0:T], ACT.Gelu_apprx_tanh).then_inc(evac, 1)

                def mat_upper(e, j):
                    act.activation(h_hi[:, j, :], unit_ap(mat, e), ACT.Copy).then_inc(m_hi, 1)

                act.wait_ge(au_used, L * (4 * U_MIX) + (4 * U_MIX + 2))
                act.wait_ge(g_used, L * N_GROUPS + (N_GROUPS + 2))
                mat_upper(0, 0)
                mat_upper(1, 1)
                with act.Fori(0, KEYS // 4 - 1) as i:
                    for j in range(4):
                        step(i + Q_V, j)
                        mat_upper(i * 4 + (j + 2), (j + 2) % 4)
                for j in range(4):
                    step(Q_PG - 1, j)
                    if j < 2:
                        mat_upper(KEYS - 2 + j, j + 2)

                act.wait_ge(x_new, L * 3 + 3)
                squares(4, x[:, :, :])
                mean_root(4)
                act.wait_ge(nt_ok, L * NORMS + 4)
                upper(h_hi[:, :, :], t_op[:, :, :])
                act.wait_ge(pe_got, L * 16 + 16)
                upper(b_hi[:, 0:CP, :], z[:, 0:CP, :])
                segment(Q_PG, 2, to_z(8, ACT.Sigmoid))
                for j in range(4):
                    step(Q_PLE, j, last=(j >= 2))
                    for k in range(2):
                        a = act.activation(z[:, 16 + 2 * j + k, :], ps[:, (2 * j + k) % 4, 0:T], ACT.Copy)
                    a.then_inc(evac, 1)
            act.wait_ge(x_new, DEPTH * 3 + 1)
            act.activation(sq, x[:, :, :], ACT.Square).then_inc(sq_ok, 1)
            act.wait_ge(ss_ok, DEPTH * NORMS + 1)
            act.activation(root[:, :], ps[:, 4, 0:T], ACT.Sqrt, bias=eps[:, 0:1], scale=1.0 / D).then_inc(rt_ok, 1)

        @block.vector
        def _(dve):
            dve.memset(ones[:, :], 1.0).then_inc(const_dve, 1)
            dve.memset(ident[:, :], 1.0).then_inc(const_dve, 1)
            dve.memset(eps[:, :], EPS).then_inc(const_dve, 1)
            for _ in range(2):
                dve.nop().then_inc(au_used, 1)
                dve.nop().then_inc(g_used, 1)
            dve.wait_ge(gains_got, 16)
            dve.wait_ge(x_got, 16)
            dve.wait_ge(const_pool, 2)
            dve.nop().then_inc(x_new, 1)

            def norm(gain_of, n, src):
                dve.wait_ge(rt_ok, n)
                dve.reciprocal(root[:, :], root[:, :])
                dve.drain()
                for c in range(C):
                    t = dve.scalar_tensor_tensor(out=t_op[:, c, :], in0=src[:, c, :], scalar=gain_of(c),
                                                 in1=root[:, :], op0=ALU.mult, op1=ALU.mult)
                t.then_inc(nt_ok, 1)
                dve.drain()

            with dve.Fori(0, DEPTH) as L:
                u0 = dve.snap(L * UNITS)

                def split(q, j):
                    dve.wait_ge(hi, u0 + q * 4 + (j + 1))
                    dve.tensor_tensor(w_lo[:, j % 2, :], raw[:, j, :], w_hi[:, j % 2, :].bitcast(F32),
                                      ALU.subtract).then_inc(lo, 1)

                def ahead(q, j):
                    split(q + (j + 2) // 4, (j + 2) % 4)

                def segment(q_first, quads):
                    dve.sem_inc(passed, 1)
                    with dve.Fori(0, quads) as i:
                        for j in range(4):
                            ahead(i + q_first, j)

                def gain(kind):
                    return lambda c: gains[:, bass.ds(L, 1), kind, c:c + 1].rearrange("p o c -> p (o c)")

                def evacuated(quads):
                    dve.wait_ge(evac, L * EVACS + (4 + 4 * quads))

                def lower(n, dst, src, upper_half):
                    dve.wait_ge(op_hi, L * PREPS + n)
                    dve.tensor_tensor(dst, src, upper_half.bitcast(F32), ALU.subtract).then_inc(op_lo, 1)

                split(0, 0)
                split(0, 1)
                norm(gain(0), L * NORMS + 1, x)
                lower(1, h_lo[:, :, :], t_op[:, :, :], h_hi[:, :, :])
                segment(0, 2)
                segment(2, 2)
                norm(gain(1), L * NORMS + 2, z)
                segment(4, 2)
                segment(6, 2)
                for g in range(GROUPS):
                    dve.wait_ge(s_ok, L * GROUPS + (g + 1))
                    dve.tensor_tensor(z[:, 8 + g, :], ps[:, 4 + g % 4, 0:T], z[:, 8 + g, :],
                                      ALU.mult).then_inc(s_used, 1)
                evacuated(8)
                dve.wait_ge(conv_got, L * 16 + 16)
                dve.memset(ext[:, :, 0:2], 0.0)
                dve.tensor_tensor(ext[:, :, 2:2 + SEQ], z[:, 16:24, 0:SEQ], z[:, 24:32, 0:SEQ], ALU.mult)
                dve.tensor_tensor(sample(ext[:, :, 2 + SEQ:EXT])[:, :, :, 2:], sample(z[:, 16:24, SEQ:T]),
                                  sample(z[:, 24:32, SEQ:T]), ALU.mult)
                dve.tensor_copy(sample(ext[:, :, 2 + SEQ:EXT])[:, :, :, 0:2], prev[:, :, :, :])
                dve.drain()
                dve.tensor_copy(after[:, :, 0:2], ext[:, :, SEQ:SEQ + 2])
                dve.tensor_copy(sample(after[:, :, 2:]), sample(ext[:, :, 2 + SEQ:EXT])[:, :, :, DEC_S:]
                                ).then_inc(cx_ok, 1)
                segment(8, 2)
                segment(10, 1)
                N = EXT - 2
                tap = flat(z[:, 16:32, :])[:, 0:C * EXT].rearrange("p (c n) -> p c n", c=C)
                for k in range(3):
                    for c in range(C):
                        w = gain(4 + k)(c)
                        if k == 0:
                            dve.tensor_scalar(tap[:, c, 0:N], ext[:, c, 0:N], w, None, ALU.mult)
                        else:
                            dve.scalar_tensor_tensor(out=tap[:, c, 0:N], in0=ext[:, c, k:k + N], scalar=w,
                                                     in1=tap[:, c, 0:N], op0=ALU.mult, op1=ALU.add)
                    dve.drain()
                evacuated(10)
                dve.tensor_tensor(z[:, 32:40, 0:SEQ], z[:, 32:40, 0:SEQ], tap[:, :, 0:SEQ], ALU.mult)
                dve.tensor_tensor(sample(z[:, 32:40, SEQ:T]), sample(z[:, 32:40, SEQ:T]),
                                  sample(tap[:, :, 2 + SEQ:EXT])[:, :, :, 0:DEC_S], ALU.mult).then_inc(ab_ok, 1)
                dve.drain()
                segment(11, 3)
                lower(2, h_lo[:, :, :], z[:, 8:16, :], h_hi[:, :, :])
                lower(3, b_lo[:, :, :], z[:, 32:40, :], b_hi[:, :, :])
                segment(Q_A, 2)
                evacuated(Q_A + 2)
                dve.tensor_tensor(z[:, 0:8, :], z[:, 0:8, :], z[:, 40:48, :], ALU.mult)
                segment(Q_B, 2)
                evacuated(Q_B + 2)
                dve.tensor_tensor(z[:, 16:24, :], z[:, 16:24, :], z[:, 48:56, :], ALU.mult)
                dve.drain()
                dve.wait_ge(out_v, L * 16 + 16)
                dve.tensor_tensor(t_op[:, :, :], z[:, 0:8, :], z[:, 16:24, :], ALU.add).then_inc(mix_ok, 1)
                lower(4, h_lo[:, :, :], t_op[:, :, :], h_hi[:, :, :])
                segment(Q_O, 2)
                evacuated(Q_O + 2)
                dve.tensor_tensor(x[:, :, :], x[:, :, :], z[:, 24:32, :], ALU.add).then_inc(x_new, 1)
                dve.drain()
                norm(gain(2), L * NORMS + 3, x)
                lower(5, h_lo[:, :, :], t_op[:, :, :], h_hi[:, :, :])
                segment(Q_Q, 4)

                def top16(pairs):
                    for dst, idx, src, spare in pairs:
                        dve.max(dst[:, 0:8], src)
                    dve.drain()
                    for dst, idx, src, spare in pairs:
                        dve.match_replace(spare, dst[:, 0:8], src, LOWEST)
                        dve.max_index(idx[:, 0:8], dst[:, 0:8], src)
                    dve.drain()
                    for dst, idx, src, spare in pairs:
                        dve.max(dst[:, 8:16], spare)
                    dve.drain()
                    for dst, idx, src, spare in pairs:
                        dve.max_index(idx[:, 8:16], dst[:, 8:16], spare)
                    dve.drain()

                def choose(pair):
                    grid = [TT, 2, TOPK, TOPK]
                    dve.tensor_copy(row[:, :, :].rearrange("p h k -> p (h k)"),
                                    scores[:, bass.ds(pair * 2, 2), :, :].rearrange("p r h k -> p (r h k)"))
                    dve.drain()
                    top16([(best[:, h, :], besti[:, h, :], row[:, h, :], cut[:, h, :]) for h in range(4)])
                    dve.tensor_copy(bestf[:, :, :], besti[:, :, :])
                    by_route = best[:, :, :].rearrange("p (r h) k -> p r h k", h=2)
                    dve.tensor_tensor(cand[:, :, :, :], by_route[:, :, 0, :].unsqueeze(3).to_broadcast(grid),
                                      by_route[:, :, 1, :].unsqueeze(2).to_broadcast(grid), ALU.add)
                    dve.drain()
                    top16([(top[:, r, :], pick[:, r, :], flat(cand[:, r, :, :]), flat(cand2[:, r, :, :]))
                           for r in range(2)])
                    ranks = pick2[:, :, :].rearrange("p (r h) k -> p r h k", h=2)
                    dve.tensor_scalar(ranks[:, :, 0, :], pick[:, :, :], 4, None, ALU.logical_shift_right)
                    dve.tensor_scalar(ranks[:, :, 1, :], pick[:, :, :], 15, None, ALU.bitwise_and)
                    dve.drain()
                    dve.tensor_copy(pickf[:, :, :], pick2[:, :, :])
                    for r in range(2):
                        dve.tensor_scalar(route[:, 2, bass.ds(pair * 2 + r, 1), :].rearrange("p o k -> p (o k)"),
                                          top[:, r, :], top[:, r, 0:1], None, ALU.subtract)
                    dve.drain()
                    grid = [TT, 4, TOPK, TOPK]
                    dve.tensor_tensor(hit[:, :, :, :], pickf[:, :, :].unsqueeze(3).to_broadcast(grid),
                                      iota[0:TT, 0:TOPK].unsqueeze(1).unsqueeze(1).to_broadcast(grid),
                                      ALU.is_equal)
                    dve.drain()
                    dve.tensor_tensor(hit[:, :, :, :], hit[:, :, :, :],
                                      bestf[:, :, :].unsqueeze(2).to_broadcast(grid), ALU.mult)
                    dve.drain()
                    for r in range(2):
                        dve.tensor_reduce(route[:, 0:2, bass.ds(pair * 2 + r, 1), :].rearrange(
                            "p h o k -> p h (o k)"), hit[:, 2 * r:2 * r + 2, :, :], AX.X, ALU.add)

                dve.wait_ge(sc_in, L * (ROUTES // 2) + ROUTES // 2)
                dve.sem_inc(passed, 1)
                with dve.Fori(0, ROUTES // 2) as pair:
                    choose(pair)
                dve.drain().then_inc(top_ok, 1)
                before = KEYS - -(-4 * (3 * TOPK + 1) * ROUTES // (4 * T)) - 1
                dve.memset(mat[:, E_MIX:before, :], 1.0)
                dve.wait_ge(ex_ok, L + 1)
                dve.tensor_reduce(total[:, :], route[:, 2, :, :], AX.X, ALU.add)
                dve.drain()
                dve.reciprocal(total[:, :], total[:, :])
                dve.drain()
                dve.tensor_tensor(route[:, 2, :, :], route[:, 2, :, :],
                                  total[:, :].unsqueeze(2).to_broadcast([TT, ROUTES, TOPK]), ALU.mult)
                dve.drain().then_inc(rt_w, 1)
                dve.wait_ge(rT_ok, L + 1)
                for k in range(3):
                    dve.tensor_copy(routeT[:, k, :], ps[:, 4 + k, 0:T])
                dve.drain().then_inc(rT_in, 1)

                def one_hots(g):
                    for k in range(GROUP):
                        dve.tensor_scalar(hot1[:, k, :], iota[:, :], routeT[:, 0, bass.ds(g * GROUP + k, 1)],
                                          routeT[:, 2, bass.ds(g * GROUP + k, 1)], ALU.is_equal, ALU.mult)
                    grid = [P, GROUP, P]
                    dve.tensor_tensor(hot2[:, :, :], iota[:, :].unsqueeze(1).to_broadcast(grid),
                                      routeT[:, 1, bass.ds(g * GROUP, GROUP)].unsqueeze(2).to_broadcast(grid),
                                      ALU.is_equal).then_inc(hot_ok, 1)

                def spread(i, last=False):
                    tile_after = {1: 0, 3: 1, 4: 2, 5: 3}
                    tiles = 0
                    for k in range(PER_QUAD):
                        g = i * PER_QUAD + k
                        dve.wait_ge(g_ok, L * N_GROUPS + g + 1)
                        if not (last and k == PER_QUAD - 1):
                            one_hots(g + 1)
                        dve.wait_ge(au_used, L * (4 * U_MIX) + i * 4 + (tiles + 2))
                        part = mat[:, :, bass.ds(g * GROUP, GROUP)]
                        dve.tensor_tensor(part, part, ps[:, 4 + k % 2, :].rearrange("p (k e) -> p e k", k=GROUP),
                                          ALU.mult).then_inc(g_used, 1)
                        if k in tile_after:
                            j = tile_after[k]
                            dve.wait_ge(evac, L * EVACS + i * 4 + (4 * (Q_U + U_TOP + U_ONLY) + 5 + j))
                            dve.wait_ge(g_used, L * N_GROUPS + g + 3)
                            tile = unit_ap(mat, i * 4 + (E_MIX + j))
                            dve.tensor_tensor(tile, tile, act_u[:, j % 2, :], ALU.mult).then_inc(au_used, 1)
                            tiles += 1

                dve.memset(mat[:, before:KEYS, :], 1.0)
                evacuated(Q_U + U_TOP + U_ONLY)
                one_hots(0)
                dve.drain()
                with dve.Fori(0, U_MIX - 1) as i:
                    spread(i)
                spread(U_MIX - 1, last=True)
                dve.drain()

                def mat_lower(e, j):
                    dve.wait_ge(m_hi, L * KEYS + e + 1)
                    dve.tensor_tensor(h_lo[:, j, :], unit_ap(mat, e), h_hi[:, j, :].bitcast(F32),
                                      ALU.subtract).then_inc(m_lo, 1)

                mat_lower(0, 0)
                mat_lower(1, 1)
                dve.wait_ge(lo, u0 + 4 * Q_V + 2)
                dve.sem_inc(passed, 1)
                with dve.Fori(0, KEYS // 4 - 1) as i:
                    for j in range(4):
                        ahead(i + Q_V, j)
                        mat_lower(i * 4 + (j + 2), (j + 2) % 4)
                for j in range(4):
                    ahead(Q_PG - 1, j)
                    if j < 2:
                        mat_lower(KEYS - 2 + j, j + 2)
                dve.wait_ge(mm, u0 + 4 * Q_PG)
                dve.wait_ge(back, L * 16 + 16)
                for c in range(C):
                    dve.tensor_tensor(x[:, c, :], x[:, c, :], ps[:, c, 0:T], ALU.add)
                dve.drain().then_inc(x_new, 1)
                norm(gain(3), L * NORMS + 4, x)
                lower(6, h_lo[:, :, :], t_op[:, :, :], h_hi[:, :, :])
                lower(7, b_lo[:, 0:CP, :], z[:, 0:CP, :], b_hi[:, 0:CP, :])
                segment(Q_PG, 2)
                for j in range(2):
                    ahead(Q_PLE, j)
                evacuated(QUADS - KEYS // 4)
                dve.tensor_tensor(z[:, 16:24, :], z[:, 16:24, :], z[:, 8:16, :], ALU.mult)
                dve.drain()
                dve.tensor_tensor(x[:, :, :], x[:, :, :], z[:, 16:24, :], ALU.add).then_inc(x_new, 1)
                dve.drain()
            norm(lambda c: gains[:, 0, 7, c:c + 1], DEPTH * NORMS + 1, x)

        @block.tensor
        def _(pe):
            pe.wait_ge(const_dve, 3)
            pe.wait_ge(const_pool, 2)

            def sum_squares(n):
                pe.wait_ge(sq_ok, n)
                for c in range(C):
                    m = pe.matmul(ps[:, 4, 0:T], ones[:, :], sq[:, c, :], start=(c == 0), stop=(c == C - 1))
                m.then_inc(ss_ok, 1)

            with pe.Fori(0, DEPTH) as L:
                u0 = pe.snap(L * UNITS)
                e0 = pe.snap(L * EVACS)

                def product(out, j, col, rhs_hi, rhs_lo, first, last):
                    wh = w_hi[:, j % 2, col:col + P]
                    wl = w_lo[:, j % 2, col:col + P]
                    pe.matmul(out, wh, rhs_hi, start=first, stop=False)
                    pe.matmul(out, wh, rhs_lo, start=False, stop=False)
                    return pe.matmul(out, wl, rhs_hi, start=False, stop=last)

                def unit(q, j, evac_q, a_hi, a_lo):
                    pe.wait_ge(lo, u0 + q * 4 + (j + 1))
                    pe.wait_ge(evac, e0 + evac_q * 4 + (j + 1))
                    for c in range(C):
                        m = product(ps[:, j, 0:T], j, c * P, a_hi[:, c, :], a_lo[:, c, :], c == 0, c == C - 1)
                    m.then_inc(mm, 1)

                def segment(q_first, quads, a_hi=h_hi, a_lo=h_lo, skipped=0):
                    pe.sem_inc(passed, 1)
                    with pe.Fori(0, quads) as i:
                        for j in range(4):
                            unit(i + q_first, j, i + (q_first - skipped), a_hi, a_lo)

                def operand(n):
                    pe.wait_ge(op_lo, L * PREPS + n)

                sum_squares(L * NORMS + 1)
                operand(1)
                segment(0, 4)
                sum_squares(L * NORMS + 2)
                segment(4, 2)
                pe.wait_ge(nt_ok, L * NORMS + 2)
                for k in range(3):
                    n = P if k < 2 else DEC
                    if k == 2:
                        pe.wait_ge(tok_ok, L * 3 + 1)
                    for c in range(C):
                        m = pe.transpose(ps[0:n, 4 + (2 * k + c // 4) % 4, c % 4 * P:c % 4 * P + P],
                                         t_op[:, c, k * P:k * P + n], ident[:, :])
                    m.then_inc(tr_ok, 1)
                segment(6, 2)
                pe.wait_ge(tok_ok, L * 3 + 3)
                pe.wait_ge(mixw_ok, L + 1)
                for g in range(GROUPS):
                    if g >= 4:
                        pe.wait_ge(s_used, L * GROUPS + (g - 3))
                    out = ps[:, 4 + g % 4, 0:T]
                    pe.matmul(out, ones[0:1, :], bias[0:1, g, :], start=True, stop=False)
                    for k in range(2):
                        pe.matmul(out[:, k * P:k * P + P], v_tok[:, k, g * P:g * P + P], ws[:, g, :],
                                  start=False, stop=False)
                    pe.matmul(out[:, SEQ:T], v_tok[0:DEC, 2, g * P:g * P + P], ws_blk[:, g, :],
                              start=False, stop=True).then_inc(s_ok, 1)
                segment(8, 6)
                operand(2)
                segment(Q_A, 2)
                operand(3)
                segment(Q_B, 2, b_hi, b_lo)
                operand(4)
                segment(Q_O, 2)
                sum_squares(L * NORMS + 3)
                operand(5)
                segment(Q_Q, 4)
                pe.wait_ge(keys_got, L * 16 + 16)
                pe.wait_ge(evac, e0 + (4 + 4 * (Q_Q + 4)))
                for r in range(ROUTES):
                    g, tile, head = r // 2, r // HEADS, r % HEADS
                    if r % 2 == 0 and g >= 4:
                        pe.wait_ge(sc_in, L * (ROUTES // 2) + (g - 3))
                    for half in range(2):
                        at = r % 2 * 2 * KEYS + half * KEYS
                        m = pe.matmul(ps[0:TT, 4 + g % 4, at:at + KEYS],
                                      z[:, 2 * head + half, tile * TT:tile * TT + TT], keys[:, half, :],
                                      start=True, stop=True)
                    if r % 2:
                        m.then_inc(sc_ok, 1)
                pe.sem_inc(passed, 1)
                with pe.Fori(0, U_TOP + U_ONLY) as i:
                    for j in range(4):
                        pe.wait_ge(evac, e0 + i * 4 + (4 * Q_U + j + 1))
                        for c in range(C):
                            if c == 0:
                                pe.wait_ge(lo_half, L * (N_FINE + 2) + i * 4 + (j + 1))
                            if c == C // 2:
                                m.then_inc(mm_half, 1)
                                pe.wait_ge(lo, u0 + i * 4 + (4 * Q_U + j + 1))
                            m = product(ps[:, j, 0:T], j, c * P, h_hi[:, c, :], h_lo[:, c, :],
                                        c == 0, c == C - 1)
                        m.then_inc(mm, 1)
                pe.wait_ge(rt_w, L + 1)
                for k in range(3):
                    for tile in range(NT):
                        m = pe.transpose(ps[:, 4 + k, tile * TT:tile * TT + TT],
                                         route[:, k, tile * HEADS:tile * HEADS + HEADS, :].rearrange("p r k -> p (r k)"),
                                         ident[0:TT, 0:TT])
                m.then_inc(rT_ok, 1)
                with pe.Fori(0, U_MIX) as i:
                    groups_at = [5, 10, 16, 21, 26, 31]
                    done, k = 0, 0
                    for j in range(4):
                        pe.wait_ge(lo, u0 + i * 4 + (4 * (Q_U + U_TOP + U_ONLY) + j + 1))
                        pe.wait_ge(evac, e0 + i * 4 + (4 * (Q_U + U_TOP + U_ONLY) + j + 1))
                        for c in range(C):
                            m = product(ps[:, j, 0:T], j, c * P, h_hi[:, c, :], h_lo[:, c, :], c == 0, c == C - 1)
                            if c == C - 1:
                                m.then_inc(mm, 1)
                            done += 1
                            if done in groups_at:
                                pe.wait_ge(hot_ok, L * N_GROUPS + i * PER_QUAD + (k + 1))
                                pe.wait_ge(g_used, L * N_GROUPS + i * PER_QUAD + (k + 1))
                                for t in range(GROUP):
                                    m = pe.matmul(ps[:, 4 + k % 2, t * P:t * P + P], hot2[:, t, :], hot1[:, t, :],
                                                  start=True, stop=True)
                                m.then_inc(g_ok, 1)
                                k += 1

                def expert_unit(q, j, e, first=False, last=False):
                    pe.wait_ge(lo, u0 + q * 4 + (j + 1))
                    pe.wait_ge(m_lo, L * KEYS + e + 1)
                    for c in range(C):
                        m = product(ps[:, c, 0:T], j, c * P, h_hi[:, j, :], h_lo[:, j, :], first, last)
                    m.then_inc(mm, 1)

                for j in range(4):
                    expert_unit(Q_V, j, j, first=(j == 0))
                with pe.Fori(1, KEYS // 4 - 1) as i:
                    for j in range(4):
                        expert_unit(i + Q_V, j, i * 4 + j)
                for j in range(4):
                    expert_unit(Q_PG - 1, j, KEYS - 4 + j, last=(j == 3))

                sum_squares(L * NORMS + 4)
                operand(6)
                segment(Q_PG, 2, skipped=KEYS // 4)
                operand(7)
                for j in range(4):
                    pe.wait_ge(lo, u0 + (4 * Q_PLE + j + 1))
                    pe.wait_ge(evac, e0 + (4 * (Q_PLE - KEYS // 4) + j + 3))
                    for k in range(2):
                        for c in range(CP):
                            m = product(ps[:, (2 * j + k) % 4, 0:T], j, (k * CP + c) * P,
                                        b_hi[:, c, :], b_lo[:, c, :], c == 0, c == CP - 1)
                    m.then_inc(mm, 1)
            sum_squares(DEPTH * NORMS + 1)


def kernel(x_prompt, x_sample, state_conv, p_prompt, p_sample, ln1, w_in, ln_v, w_s, b_s, conv_w, w_a, w_b,
           w_o, ln2, w_q, k1, k2, u_tab, v_tab, ln3, w_pg, w_ple, ln_f):
    import numpy as np
    import concourse.bacc as bacc
    from concourse.bass_utils import run_bass_kernel_spmd

    def lay(a):
        return np.ascontiguousarray(np.asarray(a))

    def tiles(w):
        w = np.asarray(w)
        k, n = w.shape
        return w.reshape(k // P, P, n // P, P).transpose(2, 1, 0, 3).reshape(n // P, P, k)

    at = {n: i * 1024 for i, n in enumerate(["u", "v", "b", "c", "x", "ga", "gb"])}
    stream = np.empty((DEPTH * UNITS, P, D), np.float32)
    for l in range(DEPTH):
        parts = []
        wi = np.asarray(w_in[l])
        for n in SEGS:
            parts.append(tiles(wi[:, at[n]:at[n] + 1024]))
        for w in (w_a, w_b, w_o, w_q):
            parts.append(tiles(w[l]))
        parts.append(tiles(np.asarray(u_tab[l]).T))
        parts.append(np.asarray(v_tab[l]).reshape(KEYS, P, D))
        parts.append(tiles(w_pg[l]))
        ple = np.zeros((4, P, D), np.float32)
        ple[:, :, 0:D // 2] = tiles(w_ple[l]).reshape(4, 2, P, CP * P).transpose(0, 2, 1, 3).reshape(4, P, D // 2)
        parts.append(ple)
        k = l * UNITS
        for p in parts:
            stream[k:k + len(p)] = p
            k += len(p)
        assert k == (l + 1) * UNITS

    def tokens(prompt, sample):
        f = prompt.shape[-1]
        a = np.concatenate([np.asarray(prompt).reshape(SEQ, f), np.asarray(sample).reshape(DEC, f)])
        return lay(a.T.reshape(f // P, P, T).transpose(1, 0, 2))

    def per_feature(a):
        return np.asarray(a).reshape(C, P).T

    gains = np.empty((P, DEPTH, 8, C), np.float32)
    for l in range(DEPTH):
        for n, g in enumerate((ln1[l], ln_v[l], ln2[l], ln3[l], conv_w[l, 0], conv_w[l, 1], conv_w[l, 2], ln_f)):
            gains[:, l, n, :] = per_feature(g)
    wsT = np.asarray(w_s).transpose(0, 3, 1, 2)
    bs = np.asarray(b_s)
    bias = np.concatenate([bs, bs] + [bs[:, :, 0:DEC_S]] * DEC_B, axis=2)
    keys = np.stack([np.asarray(k1).transpose(0, 2, 1), np.asarray(k2).transpose(0, 2, 1)], axis=2)
    conv = np.asarray(state_conv).reshape(DEPTH, DEC_B, 2, C, P).transpose(0, 4, 3, 1, 2)
    arrays = {
        "stream": stream,
        "x_in": tokens(x_prompt, x_sample),
        "pe_in": lay(np.stack([tokens(p_prompt[l], p_sample[l]) for l in range(DEPTH)])),
        "conv_in": lay(conv),
        "gains_in": gains,
        "ws_in": lay(wsT),
        "ws_blk_in": lay(wsT[:, 0:DEC_S, :, 0:DEC_S]),
        "bias_in": lay(bias),
        "keys_in": lay(keys),
    }
    nc = bacc.Bacc("TRN2", target_bir_lowering=False, num_devices=1)
    ins = [nc.dram_tensor(n, a.shape, F32, kind="ExternalInput").ap() for n, a in arrays.items()]
    shapes = {"y_out": (P, C, T), "conv_out": (DEPTH, P, C, 2 + 2 * DEC_B),
              "v_out": (DEPTH, P, C, DEC)}
    outs = [nc.dram_tensor(n, sh, F32, kind="ExternalOutput").ap() for n, sh in shapes.items()]
    hybrid_trunk(nc, *ins, *outs)
    got = run_bass_kernel_spmd(nc, [arrays], core_ids=[0]).results[0]
    y = got["y_out"].transpose(2, 1, 0).reshape(T, D)
    after = got["conv_out"]
    cp = after[:, :, :, 0:2].transpose(0, 3, 2, 1).reshape(DEPTH, 1, 2, D)
    cs = after[:, :, :, 2:].reshape(DEPTH, P, C, DEC_B, 2).transpose(0, 3, 4, 2, 1).reshape(DEPTH, DEC_B, 2, D)
    v = got["v_out"].transpose(0, 3, 2, 1).reshape(DEPTH, DEC_B, DEC_S, D)
    return (lay(y[0:SEQ].reshape(1, SEQ, D)), lay(y[SEQ:].reshape(DEC_B, DEC_S, D)), lay(cp), lay(cs), lay(v))
```

```python
import concourse.bass as bass
from concourse import mybir
from contextlib import ExitStack

P = 128
DEPTH = 2
D = 1024
C = D // P
SEQ, DEC_B, DEC_S = 256, 8, 4
DEC = DEC_B * DEC_S
T = SEQ + DEC
CHUNK = 128
GROUPS = 8
HEADS = 8
KEYS = 128
TOPK = 16
D_PLE = 256
CP = D_PLE // P
EPS = 1e-6
TT = 96
NT = T // TT
ROUTES = NT * HEADS
EXT = 2 + SEQ + DEC_B * (2 + DEC_S)

SEGS = ["v", "u", "c", "x", "b", "ga", "gb"]
Q_A = 14
Q_B = 16
Q_O = 18
Q_Q = 20
Q_U = 24
Q_V = Q_U + KEYS // 4
Q_PLE = Q_V + KEYS // 4
Q_PG = Q_PLE + 1
QUADS = Q_PG + 2
UNITS = 4 * QUADS
U_MIX = 12
GROUP = 4
N_GROUPS = T // GROUP
PER_QUAD = N_GROUPS // U_MIX
U_ONLY = 3
U_TOP = KEYS // 4 - U_ONLY - U_MIX
N_FINE = 4 * (U_TOP + U_ONLY)
E_MIX = 4 * (U_TOP + U_ONLY)
EVACS = UNITS - KEYS
NORMS = 4
SQUARES = 4 * C
LATE_FIRST = [4, 5, 6, 7, 0, 1, 2, 3]
PREPS = 8 * C + CP
T_OPS = 4 * C
X_UPS = 2 * C

F32 = mybir.dt.float32
F32R = mybir.dt.float32r
U32 = mybir.dt.uint32
ALU = mybir.AluOpType
ACT = mybir.ActivationFunctionType
AX = mybir.AxisListType
LOWEST = -3.0e38


def hybrid_trunk(nc, stream, x_in, pe_in, conv_in, gains_in, ws_in, ws_blk_in, bias_in, keys_in,
                 y_out, conv_out, v_out):
    ctx = ExitStack()
    with ctx:
        def sb(name, shape, dt, where=ctx):
            return where.enter_context(nc.sbuf_tensor(name, shape, dt))

        def sem(name):
            return ctx.enter_context(nc.semaphore(name))

        raw = sb("raw", [P, 4, D], F32)
        w_hi = sb("w_hi", [P, 2, D], F32R)
        w_lo = sb("w_lo", [P, 2, D], F32R)
        h_hi = sb("h_hi", [P, C, T], F32R)
        h_lo = sb("h_lo", [P, C, T], F32R)
        gains = sb("gains", [P, DEPTH, 8, C], F32)
        iota = sb("iota", [P, P], F32)
        ident = sb("ident", [P, P], F32)
        ones = sb("ones", [P, P], F32)
        eps = sb("eps", [P, 1], F32)
        spare = sb("spare", [P, 1], F32)
        routeT = sb("routeT", [P, 3, T], F32)
        hot1 = sb("hot1", [P, 4, P], F32)
        hot2 = sb("hot2", [P, 4, P], F32)
        act_u = sb("act_u", [P, 2, T], F32)

        front = ExitStack()
        x = sb("x", [P, C, T], F32, front)
        z = sb("z", [P, 7 * C, T], F32, front)
        t_op = sb("t_op", [P, C, T], F32, front)
        b_hi = sb("b_hi", [P, C, T], F32R, front)
        b_lo = sb("b_lo", [P, C, T], F32R, front)
        ext = sb("ext", [P, C, EXT], F32, front)
        root = sb("root", [P, T], F32, front)
        mixer = ExitStack()
        v_tok = sb("v_tok", [P, 3, D], F32, mixer)
        ws = sb("ws", [P, GROUPS, CHUNK], F32, mixer)
        ws_blk = sb("ws_blk", [DEC, GROUPS, DEC], F32, mixer)
        bias = sb("bias", [1, GROUPS, T], F32, mixer)
        prev = sb("prev", [P, C, DEC_B, 2], F32, mixer)
        after = sb("after", [P, C, 2 + 2 * DEC_B], F32, mixer)
        taps = sb("taps", [P, 3, C], F32, mixer)
        mixer.close()
        routing = ExitStack()
        scores = sb("scores", [TT, ROUTES, 2, KEYS], F32, routing)
        row = sb("row", [TT, 4, KEYS], F32, routing)
        best = sb("best", [TT, 4, TOPK], F32, routing)
        besti = sb("besti", [TT, 4, TOPK], U32, routing)
        bestf = sb("bestf", [TT, 4, TOPK], F32, routing)
        hit = sb("hit", [TT, 4, TOPK, TOPK], F32, routing)
        top = sb("top", [TT, 2, TOPK], F32, routing)
        pick = sb("pick", [TT, 2, TOPK], U32, routing)
        pick2 = sb("pick2", [TT, 4, TOPK], U32, routing)
        pickf = sb("pickf", [TT, 4, TOPK], F32, routing)
        route = sb("route", [TT, 3, ROUTES, TOPK], F32, routing)
        total = sb("total", [TT, ROUTES], F32, routing)
        routing.close()
        front.close()
        mat = sb("mat", [P, KEYS, T], F32)
        sq = ext[:, :, 0:T]
        keys = z[:, 5 * C, 0:2 * KEYS].rearrange("p (h k) -> p h k", h=2)
        cut = hit[:, 0:2, :, :].rearrange("p r (h a) b -> p (r h) (a b)", h=2)
        cand = hit[:, 2:4, :, :]
        cand2 = row[:, :, :].rearrange("p (r h) (a b) -> p r (h a) b", r=2, b=TOPK)

        ps = ctx.enter_context(nc.psum_tensor("ps", [P, 8, 512], F32))
        x_keep = nc.dram_tensor("x_keep", (P, C * T), F32, kind="Internal").ap()

        raw_in = [sem(f"raw_in{j}") for j in range(4)]
        hi = sem("hi")
        lo = sem("lo")
        mm = sem("mm")
        mm_half = sem("mm_half")
        hi_half = sem("hi_half")
        lo_half = sem("lo_half")
        evac = sem("evac")
        passed = sem("passed")
        const_dve = sem("const_dve")
        const_pool = sem("const_pool")
        gains_got = sem("gains_got")
        x_got = [sem(f"x_got{k}") for k in range(C // 2)]
        conv_got = sem("conv_got")
        mixw_got = sem("mixw_got")
        mixw_ok = sem("mixw_ok")
        pe_got = sem("pe_got")
        keys_got = sem("keys_got")
        kept = sem("kept")
        back = sem("back")
        out_v = sem("out_v")
        out_c = sem("out_c")
        out_y = sem("out_y")
        sq_ok = sem("sq_ok")
        sum_ok = sem("sum_ok")
        ss_ok = sem("ss_ok")
        rt_ok = sem("rt_ok")
        t_ok = sem("t_ok")
        conv_ok = sem("conv_ok")
        op_hi = sem("op_hi")
        op_lo = sem("op_lo")
        plus = sem("plus")
        sig = sem("sig")
        tr_ok = sem("tr_ok")
        tok_ok = sem("tok_ok")
        s_ok = sem("s_ok")
        s_used = sem("s_used")
        x_up = sem("x_up")
        cx_ok = sem("cx_ok")
        sc_ok = sem("sc_ok")
        sc_in = sem("sc_in")
        top_ok = sem("top_ok")
        ex_ok = sem("ex_ok")
        rt_w = sem("rt_w")
        rT_ok = sem("rT_ok")
        rT_in = sem("rT_in")
        hot_ok = sem("hot_ok")
        g_ok = sem("g_ok")
        g_used = sem("g_used")
        au_used = sem("au_used")
        m_hi = sem("m_hi")
        m_lo = sem("m_lo")

        block = ctx.enter_context(nc.Block())

        def flat(ap):
            return ap.rearrange("p a b -> p (a b)")

        def sample(ap):
            return ap.rearrange("p c (b s) -> p c b s", b=DEC_B)

        def unit_ap(tensor, k):
            return tensor[:, bass.ds(k, 1), :].rearrange("p o n -> p (o n)")

        @block.sync
        def _(sp):
            quads = stream.rearrange("(q j) p n -> j q p n", j=4)
            sp.dma_start(gains[:, :, :, :], gains_in).then_inc(gains_got, 16)
            for c in range(0, C, 2):
                sp.dma_start(x[:, c:c + 2, :], x_in[:, c:c + 2, :]).then_inc(x_got[c // 2], 16)
            for j in range(4):
                sp.dma_start(raw[:, j, :], quads[j, 0]).then_inc(raw_in[j], 16)
            with sp.Fori(1, DEPTH * QUADS) as q:
                free = [sp.snap(q * 4 + (j - 3)) for j in range(4)]
                for j in range(4):
                    src = quads[j][bass.ds(q, 1)].rearrange("o p n -> (o p) n")
                    sp.wait_ge(lo, free[j])
                    sp.dma_start(raw[:, j, :], src).then_inc(raw_in[j], 16)
            for j in range(2):
                sp.wait_ge(lo, DEPTH * UNITS + (j - 3))
                sp.dma_start(raw[:, j, :], quads[j, 0]).then_inc(raw_in[j], 16)

        @block.gpsimd
        def _(pool):
            pool.iota(iota[:, :], [[1, P]], base=0, channel_multiplier=0,
                      allow_small_or_imprecise_dtypes=True).then_inc(const_pool, 1)
            pool.wait_ge(const_dve, 3)
            pool.affine_select(ident[:, :], ident[:, :], [[-1, P]], ALU.is_equal, 0.0, base=0,
                               channel_multiplier=1).then_inc(const_pool, 1)

            def sum_chunks(n, order=range(C)):
                acc = sq[:, order[0], :]
                for k in range(1, C):
                    pool.wait_ge(sq_ok, n + k + 1)
                    a = pool.tensor_tensor(acc, acc, sq[:, order[k], :], ALU.add)
                    if k < C - 1:
                        pool.drain()
                a.then_inc(sum_ok, 1)

            with pool.Fori(0, DEPTH) as L:
                sum_chunks(L * SQUARES)
                pool.wait_ge(x_up, L * X_UPS + C)
                pool.sem_inc(passed, 1)
                pool.memset(ws_blk[:, :, :], 0.0)
                pool.drain()
                pool.dma_start(ws[:, :, :], ws_in[bass.ds(L, 1)].rearrange("o p g t -> (o p) g t")
                               ).then_inc(mixw_got, 16)
                pool.dma_start(bias[:, :, :], bias_in[bass.ds(L, 1)]).then_inc(mixw_got, 16)
                pool.dma_start(prev[:, :, :, :].rearrange("p c b s -> p (c b s)"),
                               conv_in[bass.ds(L, 1)].rearrange("o p c b s -> (o p) (c b s)")
                               ).then_inc(conv_got, 16)
                pool.dma_start(taps[:, :, :], gains_in[:, bass.ds(L, 1), 4:7, :].rearrange("p o k c -> p (o k) c")
                               ).then_inc(conv_got, 16)
                for b in range(DEC_B):
                    pool.dma_start(ws_blk[DEC_S * b:DEC_S * b + DEC_S, :, DEC_S * b:DEC_S * b + DEC_S],
                                   ws_blk_in[bass.ds(L, 1)].rearrange("o s g t -> (o s) g t")
                                   ).then_inc(mixw_got, 16)
                pool.wait_ge(mixw_got, L * 160 + 160)
                pool.sem_inc(passed, 1)
                pool.affine_select(ws[:, :, :], ws[:, :, :], [[0, GROUPS], [1, CHUNK]], ALU.is_ge, 0.0,
                                   base=0, channel_multiplier=-1)
                pool.affine_select(ws_blk[:, :, :], ws_blk[:, :, :], [[0, GROUPS], [1, DEC]], ALU.is_ge,
                                   0.0, base=0, channel_multiplier=-1)
                pool.drain().then_inc(mixw_ok, 1)
                sum_chunks(L * SQUARES + C)
                pool.wait_ge(t_ok, L * T_OPS + 2 * C)
                pool.sem_inc(passed, 1)
                pool.dma_start(v_out[bass.ds(L, 1)].rearrange("o p c t -> (o p) c t"),
                               t_op[:, :, SEQ:T]).then_inc(out_v, 16)

                pool.wait_ge(evac, L * EVACS + (4 + 4 * 8))
                pool.sem_inc(passed, 1)
                pool.wait_ge(conv_got, L * 32 + 32)
                pool.sem_inc(passed, 1)
                pool.memset(ext[:, :, 0:2], 0.0)
                pool.tensor_tensor(ext[:, :, 2:2 + SEQ], z[:, 16:24, 0:SEQ], z[:, 24:32, 0:SEQ], ALU.mult)
                pool.tensor_tensor(sample(ext[:, :, 2 + SEQ:EXT])[:, :, :, 2:], sample(z[:, 16:24, SEQ:T]),
                                   sample(z[:, 24:32, SEQ:T]), ALU.mult)
                pool.tensor_copy(sample(ext[:, :, 2 + SEQ:EXT])[:, :, :, 0:2], prev[:, :, :, :])
                pool.drain()
                pool.tensor_copy(after[:, :, 0:2], ext[:, :, SEQ:SEQ + 2])
                pool.tensor_copy(sample(after[:, :, 2:]), sample(ext[:, :, 2 + SEQ:EXT])[:, :, :, DEC_S:])
                for k, at in enumerate((16, 24, 0)):
                    for c in range(C):
                        w = taps[:, k, c:c + 1]
                        pool.tensor_scalar(z[:, at + c, 0:SEQ], ext[:, c, k:k + SEQ], w, None, ALU.mult)
                        pool.tensor_scalar(z[:, at + c, SEQ:T].rearrange("p (b s) -> p b s", b=DEC_B),
                                           sample(ext[:, :, 2 + SEQ:EXT])[:, c, :, k:k + DEC_S], w, None, ALU.mult)
                pool.drain().then_inc(cx_ok, 1)
                pool.wait_ge(cx_ok, L + 1)
                pool.sem_inc(passed, 1)
                pool.dma_start(conv_out[bass.ds(L, 1)].rearrange("o p c s -> (o p) (c s)"),
                               flat(after[:, :, :])).then_inc(out_c, 16)
                pool.tensor_tensor(z[:, 16:24, :], z[:, 16:24, :], z[:, 24:32, :], ALU.add)
                pool.drain()
                pool.tensor_tensor(z[:, 16:24, :], z[:, 16:24, :], z[:, 0:8, :], ALU.add)
                pool.drain()
                pool.wait_ge(evac, L * EVACS + (4 + 4 * 10))
                pool.sem_inc(passed, 1)
                pool.tensor_tensor(z[:, 32:40, :], z[:, 32:40, :], z[:, 16:24, :], ALU.mult).then_inc(conv_ok, 1)
                pool.wait_ge(t_ok, L * T_OPS + 3 * C)
                pool.sem_inc(passed, 1)
                pool.dma_start(keys[:, :, :], keys_in[bass.ds(L, 1)].rearrange("o p h k -> (o p) h k")
                               ).then_inc(keys_got, 16)
                sum_chunks(L * SQUARES + 2 * C)
                pool.wait_ge(evac, L * EVACS + (4 + 4 * Q_Q))
                pool.sem_inc(passed, 1)
                pool.dma_start(x_keep, flat(x[:, :, :])).then_inc(kept, 16)
                pool.wait_ge(lo, L * UNITS + 4 * Q_U + 2)
                pool.sem_inc(passed, 1)
                pool.sem_inc(lo_half, 2)

                def lower(k, lo_col, hi_col):
                    return pool.tensor_tensor(w_lo[:, k % 2, lo_col:hi_col], raw[:, k, lo_col:hi_col],
                                              w_hi[:, k % 2, lo_col:hi_col].bitcast(F32), ALU.subtract)

                with pool.Fori(0, U_TOP + U_ONLY) as i:
                    for j in range(4):
                        pool.wait_ge(hi_half, L * N_FINE + i * 4 + (j + 1))
                        lower((j + 2) % 4, 0, D // 2).then_inc(lo_half, 1)
                        pool.wait_ge(hi, L * UNITS + i * 4 + (4 * Q_U + j + 3))
                        lower((j + 2) % 4, D // 2, D).then_inc(lo, 1)
                with pool.Fori(Q_V - U_MIX, Q_V) as q:
                    for j in range(4):
                        pool.wait_ge(hi, L * UNITS + q * 4 + (j + 3))
                        lower((j + 2) % 4, 0, D).then_inc(lo, 1)
                pool.wait_ge(au_used, L * (4 * U_MIX) + (4 * U_MIX + 2))
                pool.sem_inc(passed, 1)
                pool.dma_start(act_u[:, :, :], pe_in[bass.ds(L, 1)].rearrange("o p c t -> (o p) c t")
                               ).then_inc(pe_got, 16)
                pool.wait_ge(m_lo, L * KEYS + C)
                pool.sem_inc(passed, 1)
                pool.dma_start(flat(x[:, :, :]), x_keep).then_inc(back, 16)
                sum_chunks(L * SQUARES + 3 * C, LATE_FIRST)
            sum_chunks(DEPTH * SQUARES)
            for half in range(2):
                pool.wait_ge(t_ok, DEPTH * T_OPS + (half + 1) * (C // 2))
                pool.dma_start(y_out[:, half * (C // 2):(half + 1) * (C // 2), :],
                               t_op[:, half * (C // 2):(half + 1) * (C // 2), :]).then_inc(out_y, 16)
            pool.wait_ge(out_v, 16 * DEPTH)
            pool.wait_ge(out_c, 16 * DEPTH)
            pool.wait_ge(kept, 16 * DEPTH)
            pool.wait_ge(out_y, 32)

        @block.scalar
        def _(act):
            for _ in range(4):
                act.nop().then_inc(evac, 1)
            act.wait_ge(const_dve, 3)

            def squares(c):
                act.activation(sq[:, c, :], x[:, c, :], ACT.Square).then_inc(sq_ok, 1)

            act.wait_ge(gains_got, 16)
            for c in range(C):
                act.wait_ge(x_got[c // 2], 16)
                act.activation(h_hi[:, c, :], x[:, c, :], ACT.Copy, scale=gains[:, 0, 0, c:c + 1]).then_inc(op_hi, 1)
            for j in range(2):
                act.wait_ge(raw_in[j], 16)
                act.activation(w_hi[:, j, :], raw[:, j, :], ACT.Copy).then_inc(hi, 1)
            for c in range(C):
                squares(c)
            with act.Fori(0, DEPTH) as L:
                q0 = act.snap(L * QUADS)
                u0 = act.snap(L * UNITS)

                def split(q, j):
                    act.wait_ge(raw_in[j], (q0 + q) * 16 + 16)
                    act.activation(w_hi[:, j % 2, :], raw[:, j, :], ACT.Copy).then_inc(hi, 1)

                def segment(q_first, quads, evacuate):
                    with act.Fori(0, quads) as i:
                        for j in range(4):
                            act.wait_ge(mm, u0 + i * 4 + (4 * q_first + j + 1))
                            evacuate(i, j).then_inc(evac, 1)
                            split(i + (q_first + (j + 2) // 4), (j + 2) % 4)

                def fine_segment(first, quads):
                    with act.Fori(first, first + quads) as i:
                        for j in range(4):
                            k = (j + 2) % 4
                            act.wait_ge(mm_half, L * N_FINE + i * 4 + (j + 1))
                            act.wait_ge(raw_in[k], (q0 + i) * 16 + (16 * (Q_U + (j + 2) // 4) + 16))
                            act.activation(w_hi[:, k % 2, 0:D // 2], raw[:, k, 0:D // 2], ACT.Copy
                                           ).then_inc(hi_half, 1)
                            act.wait_ge(mm, u0 + i * 4 + (4 * Q_U + j + 1))
                            act.activation(w_hi[:, k % 2, D // 2:D], raw[:, k, D // 2:D], ACT.Copy
                                           ).then_inc(hi, 1)
                            act.activation(unit_ap(mat, i * 4 + j), ps[:, j, 0:T], ACT.Gelu_apprx_tanh
                                           ).then_inc(evac, 1)

                def bring_table(func):
                    act.activation(spare[:, :], eps[:, :], func)

                def mean_root(n):
                    bring_table(ACT.Sqrt)
                    act.wait_ge(ss_ok, L * NORMS + n)
                    act.activation(root[:, :], ps[:, 4, 0:T], ACT.Sqrt, bias=eps[:, 0:1],
                                   scale=1.0 / D).then_inc(rt_ok, 1)

                def upper(dst, src, scale=1.0):
                    act.activation(dst, src, ACT.Copy, scale=scale).then_inc(op_hi, 1)

                def gain(kind, c):
                    return gains[:, :, :, :].rearrange("p l k c -> p (l k c)")[:, bass.ds(L * (8 * C) + kind * C + c, 1)]

                def emptied(n):
                    act.wait_ge(evac, L * EVACS + (n + 5))

                def to_z(first, func):
                    def evacuate(i, j):
                        return act.activation(unit_ap(z, i * 4 + (first + j)), ps[:, j, 0:T], func)
                    return evacuate

                def step(q, j):
                    act.wait_ge(mm, u0 + q * 4 + (j + 1))
                    split(q + (j + 2) // 4, (j + 2) % 4)

                def gelu(n):
                    emptied(n)
                    return act.activation(unit_ap(z, n), unit_ap(z, n), ACT.Gelu_apprx_tanh)

                step(0, 0)
                step(0, 1)
                mean_root(1)
                gelu(0)
                gelu(1)
                for j in (2, 3):
                    step(0, j)
                    gelu(j)
                for j in range(4):
                    step(1, j)
                    gelu(4 + j)
                act.drain()
                with act.Fori(0, 2) as i:
                    for j in range(4):
                        step(i + 2, j)
                        gelu(i * 4 + (8 + j))
                        act.wait_ge(t_ok, L * T_OPS + i * 4 + (j + 1))
                        upper(unit_ap(b_hi, i * 4 + j), unit_ap(t_op, i * 4 + j))
                        act.activation(unit_ap(sq, i * 4 + j), unit_ap(z, i * 4 + j), ACT.Square).then_inc(sq_ok, 1)
                step(4, 0)
                step(4, 1)
                mean_root(2)
                for j in range(4):
                    if j >= 2:
                        step(4, j)
                    act.activation(z[:, 16 + j, :], ps[:, j, 0:T], ACT.Copy).then_inc(evac, 1)
                segment(5, 1, to_z(20, ACT.Copy))
                for k in range(3):
                    act.wait_ge(tr_ok, L * 3 + (k + 1))
                    for half in range(2):
                        rows = P if k < 2 else DEC
                        a = act.activation(v_tok[0:rows, k, half * 512:half * 512 + 512],
                                           ps[0:rows, 4 + (2 * k + half) % 4, :], ACT.Copy)
                    a.then_inc(tok_ok, 1)
                segment(6, 2, to_z(24, ACT.Copy))
                for c in range(C):
                    act.wait_ge(s_used, L * GROUPS + (c + 1))
                    upper(h_hi[:, c, :], z[:, 8 + c, :])
                segment(8, 2, to_z(32, ACT.Copy))
                bring_table(ACT.Sigmoid)
                segment(10, 4, to_z(40, ACT.Sigmoid))
                act.wait_ge(conv_ok, L + 1)
                act.sem_inc(passed, 1)
                with act.Fori(0, 2) as i:
                    for j in range(4):
                        step(i + Q_A, j)
                        upper(unit_ap(b_hi, i * 4 + j), unit_ap(z, i * 4 + (32 + j)))
                with act.Fori(0, 2) as i:
                    for j in range(4):
                        step(i + Q_B, j)
                        act.wait_ge(t_ok, L * T_OPS + i * 4 + (2 * C + j + 1))
                        upper(unit_ap(h_hi, i * 4 + j), unit_ap(t_op, i * 4 + j))
                for c in range(C):
                    step(Q_O + c // 4, c % 4)
                    emptied(4 * Q_O + c)
                    upper(b_hi[:, c, :], x[:, c, :], gain(2, c))
                    squares(c)
                step(Q_Q, 0)
                step(Q_Q, 1)
                mean_root(3)
                step(Q_Q, 2)
                step(Q_Q, 3)
                with act.Fori(0, 2) as i:
                    for j in range(4):
                        step(i + (Q_Q + 1), j)
                        act.wait_ge(t_ok, L * T_OPS + i * 4 + (3 * C + j + 1))
                        upper(unit_ap(h_hi, i * 4 + j), unit_ap(t_op, i * 4 + j))
                for j in range(4):
                    step(Q_Q + 3, j)
                act.wait_ge(out_c, L * 16 + 16)
                for g in range(ROUTES // 2):
                    act.wait_ge(sc_ok, L * (ROUTES // 2) + (g + 1))
                    act.activation(scores[:, 2 * g:2 * g + 2, :, :].rearrange("p a b k -> p (a b k)"),
                                   ps[0:TT, 4 + g % 4, :], ACT.Copy).then_inc(sc_in, 1)

                act.wait_ge(kept, L * 16 + 16)
                bring_table(ACT.Gelu_apprx_tanh)
                fine_segment(0, U_TOP)
                act.wait_ge(top_ok, L + 1)
                act.activation(route[:, 2, :, :], route[:, 2, :, :], ACT.Exp).then_inc(ex_ok, 1)

                bring_table(ACT.Gelu_apprx_tanh)
                fine_segment(U_TOP, U_ONLY)
                with act.Fori(0, U_MIX) as i:
                    for j in range(4):
                        step(i + (Q_U + U_TOP + U_ONLY), j)
                        act.wait_ge(au_used, L * (4 * U_MIX) + i * 4 + (j + 1))
                        act.activation(act_u[:, j % 2, :], ps[:, j, 0:T], ACT.Gelu_apprx_tanh).then_inc(evac, 1)

                def mat_upper(e, j):
                    act.activation(h_hi[:, j, :], unit_ap(mat, e), ACT.Copy).then_inc(m_hi, 1)

                act.wait_ge(g_used, L * N_GROUPS + (N_GROUPS + 2))
                for j in range(3):
                    mat_upper(j, j)
                act.wait_ge(au_used, L * (4 * U_MIX) + (4 * U_MIX + 2))
                act.sem_inc(passed, 1)
                with act.Fori(0, KEYS // 4 - 1) as i:
                    for j in range(4):
                        step(i + Q_V, j)
                        mat_upper(i * 4 + (j + 3), (j + 3) % 4)
                act.wait_ge(pe_got, L * 16 + 16)
                for c in range(CP):
                    upper(h_hi[:, 4 + c, :], act_u[:, c, :])
                for j in range(4):
                    step(Q_PLE - 1, j)
                    if j == 0:
                        mat_upper(KEYS - 1, 3)

                def gained(k):
                    act.wait_ge(x_up, L * X_UPS + (C + k + 1))
                    upper(b_hi[:, LATE_FIRST[k], :], x[:, LATE_FIRST[k], :], gain(3, LATE_FIRST[k]))

                for k in range(4):
                    gained(k)
                for k in range(4):
                    squares(LATE_FIRST[k])
                for j in range(4):
                    step(Q_PLE, j)
                    for c in (2 * j, 2 * j + 1):
                        a = act.activation(z[:, c, :], ps[:, 4 + c % 4, 0:T], ACT.Copy)
                    a.then_inc(evac, 1)
                    for k in (2 * j, 2 * j + 1):
                        if j < 2:
                            gained(4 + k)
                        else:
                            squares(LATE_FIRST[k])

                def sigmoid(c):
                    emptied(4 * (Q_PG - KEYS // 4) + c)
                    act.activation(z[:, 8 + c, :], z[:, 8 + c, :], ACT.Sigmoid).then_inc(sig, 1)

                def next_operand(c):
                    act.wait_ge(x_up, L * X_UPS + (2 * C + c + 1))
                    upper(h_hi[:, c, :], x[:, c, :], gain(7, c))
                    squares(c)

                step(Q_PG, 0)
                step(Q_PG, 1)
                mean_root(4)
                sigmoid(0)
                sigmoid(1)
                for c in range(2, C):
                    step(Q_PG + c // 4, c % 4)
                    sigmoid(c)
                    next_operand(c - 2)
                next_operand(C - 2)
                next_operand(C - 1)
            act.activation(spare[:, :], eps[:, :], ACT.Sqrt)
            act.wait_ge(ss_ok, DEPTH * NORMS + 1)
            act.activation(root[:, :], ps[:, 4, 0:T], ACT.Sqrt, bias=eps[:, 0:1], scale=1.0 / D).then_inc(rt_ok, 1)

        @block.vector
        def _(dve):
            dve.memset(ones[:, :], 1.0).then_inc(const_dve, 1)
            dve.memset(ident[:, :], 1.0).then_inc(const_dve, 1)
            dve.memset(eps[:, :], EPS).then_inc(const_dve, 1)
            for _ in range(2):
                dve.nop().then_inc(au_used, 1)
                dve.nop().then_inc(g_used, 1)
            dve.wait_ge(gains_got, 16)
            dve.sem_inc(x_up, C)
            for c in range(C):
                dve.wait_ge(op_hi, c + 1)
                dve.scalar_tensor_tensor(out=h_lo[:, c, :], in0=x[:, c, :], scalar=gains[:, 0, 0, c:c + 1],
                                         in1=h_hi[:, c, :].bitcast(F32), op0=ALU.mult, op1=ALU.subtract
                                         ).then_inc(op_lo, 1)

            for j in range(2):
                dve.wait_ge(hi, j + 1)
                dve.tensor_tensor(w_lo[:, j, :], raw[:, j, :], w_hi[:, j, :].bitcast(F32),
                                  ALU.subtract).then_inc(lo, 1)
            dve.wait_ge(const_pool, 2)
            with dve.Fori(0, DEPTH) as L:
                u0 = dve.snap(L * UNITS)

                def split(q, j):
                    dve.wait_ge(hi, u0 + q * 4 + (j + 1))
                    dve.tensor_tensor(w_lo[:, j % 2, :], raw[:, j, :], w_hi[:, j % 2, :].bitcast(F32),
                                      ALU.subtract).then_inc(lo, 1)

                def ahead(q, j):
                    split(q + (j + 2) // 4, (j + 2) % 4)

                def segment(q_first, quads):
                    dve.sem_inc(passed, 1)
                    with dve.Fori(0, quads) as i:
                        for j in range(4):
                            ahead(i + q_first, j)

                def gain(kind, c):
                    return gains[:, :, :, :].rearrange("p l k c -> p (l k c)")[:, bass.ds(L * (8 * C) + kind * C + c, 1)]

                def evacuated(quads):
                    dve.wait_ge(evac, L * EVACS + (4 + 4 * quads))

                def inverse_root(n):
                    dve.wait_ge(rt_ok, L * NORMS + n)
                    dve.reciprocal(root[:, :], root[:, :])
                    dve.drain()

                def normalised(kind, c, src):
                    dve.scalar_tensor_tensor(out=unit_ap(t_op, c), in0=unit_ap(src, c), scalar=gain(kind, c),
                                             in1=root[:, :], op0=ALU.mult, op1=ALU.mult).then_inc(t_ok, 1)

                def lower(n, c, hi_of, lo_of, src):
                    dve.wait_ge(op_hi, L * PREPS + n + 1)
                    dve.tensor_tensor(unit_ap(lo_of, c), unit_ap(src, c), unit_ap(hi_of, c).bitcast(F32),
                                      ALU.subtract).then_inc(op_lo, 1)

                def lower_scaled(n, c, kind, hi_of, lo_of):
                    dve.wait_ge(op_hi, L * PREPS + n + 1)
                    dve.scalar_tensor_tensor(out=lo_of[:, c, :], in0=x[:, c, :], scalar=gain(kind, c),
                                             in1=hi_of[:, c, :].bitcast(F32), op0=ALU.mult, op1=ALU.subtract
                                             ).then_inc(op_lo, 1)

                def evacuate(q, j, dst, factor):
                    dve.wait_ge(mm, u0 + q * 4 + (j + 1))
                    dve.tensor_tensor(dst, ps[:, j, 0:T], factor, ALU.mult).then_inc(evac, 1)

                ahead(0, 0)
                ahead(0, 1)
                inverse_root(1)
                evacuate(0, 0, z[:, 0, :], root[:, :])
                evacuate(0, 1, z[:, 1, :], root[:, :])
                for n in range(2, 8):
                    evacuate(n // 4, n % 4, z[:, n, :], root[:, :])
                    ahead(n // 4, n % 4)
                with dve.Fori(0, 2) as i:
                    for j in range(4):
                        evacuate(i + 2, j, unit_ap(z, i * 4 + (8 + j)), root[:, :])
                        normalised(0, i * 4 + j, x)
                        ahead(i + 2, j)
                        lower(i * 4 + (C + j), i * 4 + j, b_hi, b_lo, t_op)
                ahead(4, 0)
                ahead(4, 1)
                inverse_root(2)
                for n in range(2, 8):
                    ahead(4 + n // 4, n % 4)
                    if n < 6:
                        for c in (2 * n - 4, 2 * n - 3):
                            normalised(1, c, z)
                segment(6, 2)
                for g in range(GROUPS):
                    dve.wait_ge(s_ok, L * GROUPS + (g + 1))
                    dve.tensor_tensor(z[:, 8 + g, :], ps[:, 4 + g % 4, 0:T], z[:, 8 + g, :],
                                      ALU.mult).then_inc(s_used, 1)
                for c in range(C):
                    dve.wait_ge(op_hi, L * PREPS + (2 * C + c + 1))
                    dve.tensor_tensor(h_lo[:, c, :], z[:, 8 + c, :], h_hi[:, c, :].bitcast(F32),
                                      ALU.subtract).then_inc(op_lo, 1)
                segment(8, 6)
                evacuated(Q_A)
                dve.sem_inc(passed, 1)
                with dve.Fori(0, 2) as i:
                    for j in range(4):
                        evacuate(i + Q_A, j, unit_ap(z, i * 4 + (40 + j)), unit_ap(z, i * 4 + (40 + j)))
                        ahead(i + Q_A, j)
                        dve.wait_ge(op_hi, L * PREPS + i * 4 + (3 * C + j + 1))
                        dve.tensor_tensor(unit_ap(b_lo, i * 4 + j), unit_ap(z, i * 4 + (32 + j)),
                                          unit_ap(b_hi, i * 4 + j).bitcast(F32), ALU.subtract).then_inc(op_lo, 1)
                dve.wait_ge(out_v, L * 16 + 16)
                dve.sem_inc(passed, 1)
                with dve.Fori(0, 2) as i:
                    for j in range(4):
                        evacuate(i + Q_B, j, unit_ap(t_op, i * 4 + j), unit_ap(z, i * 4 + (48 + j)))
                        ahead(i + Q_B, j)
                        dve.wait_ge(evac, L * EVACS + i * 4 + (4 * Q_B + j + 5))
                        dve.tensor_tensor(unit_ap(t_op, i * 4 + j), unit_ap(t_op, i * 4 + j),
                                          unit_ap(z, i * 4 + (40 + j)), ALU.add).then_inc(t_ok, 1)
                        lower(i * 4 + (4 * C + j), i * 4 + j, h_hi, h_lo, t_op)
                for c in range(C):
                    dve.wait_ge(mm, u0 + (4 * Q_O + c + 1))
                    dve.tensor_tensor(x[:, c, :], x[:, c, :], ps[:, c % 4, 0:T], ALU.add).then_inc(evac, 1)
                    ahead(Q_O + c // 4, c % 4)
                    lower_scaled(5 * C + c, c, 2, b_hi, b_lo)
                ahead(Q_Q, 0)
                ahead(Q_Q, 1)
                inverse_root(3)
                evacuate(Q_Q, 0, z[:, 0, :], root[:, :])
                evacuate(Q_Q, 1, z[:, 1, :], root[:, :])
                for j in (2, 3):
                    evacuate(Q_Q, j, z[:, j, :], root[:, :])
                    ahead(Q_Q, j)
                with dve.Fori(0, 2) as i:
                    for j in range(4):
                        evacuate(i + (Q_Q + 1), j, unit_ap(z, i * 4 + (4 + j)), root[:, :])
                        normalised(2, i * 4 + j, x)
                        ahead(i + (Q_Q + 1), j)
                        lower(i * 4 + (6 * C + j), i * 4 + j, h_hi, h_lo, t_op)
                for j in range(4):
                    evacuate(Q_Q + 3, j, z[:, 12 + j, :], root[:, :])
                    ahead(Q_Q + 3, j)

                def top16(pairs):
                    for dst, idx, src, spare in pairs:
                        dve.max(dst[:, 0:8], src)
                    dve.drain()
                    for dst, idx, src, spare in pairs:
                        dve.match_replace(spare, dst[:, 0:8], src, LOWEST)
                        dve.max_index(idx[:, 0:8], dst[:, 0:8], src)
                    dve.drain()
                    for dst, idx, src, spare in pairs:
                        dve.max(dst[:, 8:16], spare)
                    dve.drain()
                    for dst, idx, src, spare in pairs:
                        dve.max_index(idx[:, 8:16], dst[:, 8:16], spare)
                    dve.drain()

                def choose(pair):
                    grid = [TT, 2, TOPK, TOPK]
                    dve.tensor_copy(row[:, :, :].rearrange("p h k -> p (h k)"),
                                    scores[:, bass.ds(pair * 2, 2), :, :].rearrange("p r h k -> p (r h k)"))
                    dve.drain()
                    top16([(best[:, h, :], besti[:, h, :], row[:, h, :], cut[:, h, :]) for h in range(4)])
                    dve.tensor_copy(bestf[:, :, :], besti[:, :, :])
                    by_route = best[:, :, :].rearrange("p (r h) k -> p r h k", h=2)
                    dve.tensor_tensor(cand[:, :, :, :], by_route[:, :, 0, :].unsqueeze(3).to_broadcast(grid),
                                      by_route[:, :, 1, :].unsqueeze(2).to_broadcast(grid), ALU.add)
                    dve.drain()
                    top16([(top[:, r, :], pick[:, r, :], flat(cand[:, r, :, :]), flat(cand2[:, r, :, :]))
                           for r in range(2)])
                    ranks = pick2[:, :, :].rearrange("p (r h) k -> p r h k", h=2)
                    dve.tensor_scalar(ranks[:, :, 0, :], pick[:, :, :], 4, None, ALU.logical_shift_right)
                    dve.tensor_scalar(ranks[:, :, 1, :], pick[:, :, :], 15, None, ALU.bitwise_and)
                    dve.drain()
                    dve.tensor_copy(pickf[:, :, :], pick2[:, :, :])
                    for r in range(2):
                        dve.tensor_scalar(route[:, 2, bass.ds(pair * 2 + r, 1), :].rearrange("p o k -> p (o k)"),
                                          top[:, r, :], top[:, r, 0:1], None, ALU.subtract)
                    dve.drain()
                    grid = [TT, 4, TOPK, TOPK]
                    dve.tensor_tensor(hit[:, :, :, :], pickf[:, :, :].unsqueeze(3).to_broadcast(grid),
                                      iota[0:TT, 0:TOPK].unsqueeze(1).unsqueeze(1).to_broadcast(grid),
                                      ALU.is_equal)
                    dve.drain()
                    dve.tensor_tensor(hit[:, :, :, :], hit[:, :, :, :],
                                      bestf[:, :, :].unsqueeze(2).to_broadcast(grid), ALU.mult)
                    dve.drain()
                    for r in range(2):
                        dve.tensor_reduce(route[:, 0:2, bass.ds(pair * 2 + r, 1), :].rearrange(
                            "p h o k -> p h (o k)"), hit[:, 2 * r:2 * r + 2, :, :], AX.X, ALU.add)

                dve.wait_ge(sc_in, L * (ROUTES // 2) + ROUTES // 2)
                dve.sem_inc(passed, 1)
                with dve.Fori(0, ROUTES // 2) as pair:
                    choose(pair)
                dve.drain().then_inc(top_ok, 1)
                before = KEYS - -(-4 * (3 * TOPK + 1) * ROUTES // (4 * T)) - 1
                dve.memset(mat[:, E_MIX:before, :], 1.0)
                dve.wait_ge(ex_ok, L + 1)
                dve.tensor_reduce(total[:, :], route[:, 2, :, :], AX.X, ALU.add)
                dve.drain()
                dve.reciprocal(total[:, :], total[:, :])
                dve.drain()
                dve.tensor_tensor(route[:, 2, :, :], route[:, 2, :, :],
                                  total[:, :].unsqueeze(2).to_broadcast([TT, ROUTES, TOPK]), ALU.mult)
                dve.drain().then_inc(rt_w, 1)
                dve.wait_ge(rT_ok, L + 1)
                for k in range(3):
                    dve.tensor_copy(routeT[:, k, :], ps[:, 4 + k, 0:T])
                dve.drain().then_inc(rT_in, 1)

                def one_hots(g, half):
                    k = 2 * half
                    grid = [P, 2, P]
                    dve.tensor_tensor(hot2[:, k:k + 2, :], iota[:, :].unsqueeze(1).to_broadcast(grid),
                                      routeT[:, 1, bass.ds(g * GROUP + k, 2)].unsqueeze(2).to_broadcast(grid),
                                      ALU.is_equal)
                    for t in (k, k + 1):
                        h = dve.tensor_scalar(hot1[:, t, :], iota[:, :], routeT[:, 0, bass.ds(g * GROUP + t, 1)],
                                              routeT[:, 2, bass.ds(g * GROUP + t, 1)], ALU.is_equal, ALU.mult)
                    h.then_inc(hot_ok, 1)

                def spread(i, last=False):
                    tile_after = {1: 0, 3: 1, 4: 2, 5: 3}
                    tiles = 0
                    for k in range(PER_QUAD):
                        g = i * PER_QUAD + k
                        for half in range(2):
                            dve.wait_ge(g_ok, 2 * (L * N_GROUPS + g) + (half + 1))
                            if not (last and k == PER_QUAD - 1):
                                one_hots(g + 1, half)
                        dve.wait_ge(au_used, L * (4 * U_MIX) + i * 4 + (tiles + 2))
                        part = mat[:, :, bass.ds(g * GROUP, GROUP)]
                        dve.tensor_tensor(part, part, ps[:, 4 + k % 2, :].rearrange("p (k e) -> p e k", k=GROUP),
                                          ALU.mult).then_inc(g_used, 1)
                        if k in tile_after:
                            j = tile_after[k]
                            dve.wait_ge(evac, L * EVACS + i * 4 + (4 * (Q_U + U_TOP + U_ONLY) + 5 + j))
                            dve.wait_ge(g_used, L * N_GROUPS + g + 3)
                            tile = unit_ap(mat, i * 4 + (E_MIX + j))
                            dve.tensor_tensor(tile, tile, act_u[:, j % 2, :], ALU.mult).then_inc(au_used, 1)
                            tiles += 1

                dve.memset(mat[:, before:KEYS, :], 1.0)
                evacuated(Q_U + U_TOP + U_ONLY)
                one_hots(0, 0)
                one_hots(0, 1)
                dve.drain()
                with dve.Fori(0, U_MIX - 1) as i:
                    spread(i)
                spread(U_MIX - 1, last=True)

                def mat_lower(e, j):
                    dve.wait_ge(m_hi, L * KEYS + e + 1)
                    dve.tensor_tensor(h_lo[:, j, :], unit_ap(mat, e), h_hi[:, j, :].bitcast(F32),
                                      ALU.subtract).then_inc(m_lo, 1)

                for j in range(3):
                    mat_lower(j, j)
                dve.wait_ge(lo, u0 + 4 * Q_V + 2)
                dve.sem_inc(passed, 1)
                with dve.Fori(0, KEYS // 4 - 1) as i:
                    for j in range(4):
                        ahead(i + Q_V, j)
                        mat_lower(i * 4 + (j + 3), (j + 3) % 4)
                for c in range(CP):
                    dve.wait_ge(op_hi, L * PREPS + (7 * C + c + 1))
                    dve.tensor_tensor(h_lo[:, 4 + c, :], act_u[:, c, :], h_hi[:, 4 + c, :].bitcast(F32),
                                      ALU.subtract).then_inc(op_lo, 1)
                for j in range(3):
                    ahead(Q_PLE - 1, j)
                    if j == 0:
                        mat_lower(KEYS - 1, 3)

                dve.wait_ge(mm, u0 + 4 * Q_PLE)
                dve.wait_ge(back, L * 16 + 16)
                dve.sem_inc(passed, 1)
                for k, c in enumerate(LATE_FIRST):
                    if k == 4:
                        ahead(Q_PLE - 1, 3)
                    dve.tensor_tensor(x[:, c, :], x[:, c, :], ps[:, c, 0:T], ALU.add).then_inc(x_up, 1)
                for j in range(4):
                    for k in (2 * j, 2 * j + 1):
                        lower_scaled(7 * C + CP + k, LATE_FIRST[k], 3, b_hi, b_lo)
                    ahead(Q_PLE, j)

                def gate(c):
                    dve.wait_ge(sig, L * C + (c + 1))
                    dve.tensor_tensor(z[:, 8 + c, :], z[:, 8 + c, :], z[:, c, :], ALU.mult).then_inc(plus, 1)

                def add_gated(c):
                    dve.wait_ge(plus, L * C + (c + 1))
                    dve.tensor_tensor(x[:, c, :], x[:, c, :], z[:, 8 + c, :], ALU.add).then_inc(x_up, 1)

                def next_lower(c):
                    lower_scaled(8 * C + CP + c, c, 7, h_hi, h_lo)

                ahead(Q_PG, 0)
                ahead(Q_PG, 1)
                inverse_root(4)
                for c in range(C):
                    evacuate(Q_PG + c // 4, c % 4, z[:, 8 + c, :], root[:, :])
                    if c >= 2:
                        ahead(Q_PG + c // 4, c % 4)
                    if c >= 1:
                        gate(c - 1)
                    if c >= 3:
                        next_lower(c - 3)
                    if c >= 1:
                        add_gated(c - 1)
                next_lower(C - 3)
                gate(C - 1)
                next_lower(C - 2)
                add_gated(C - 1)
                next_lower(C - 1)
            dve.wait_ge(rt_ok, DEPTH * NORMS + 1)
            dve.reciprocal(root[:, :], root[:, :])
            dve.drain()
            for c in range(C):
                dve.scalar_tensor_tensor(out=t_op[:, c, :], in0=x[:, c, :], scalar=gains[:, DEPTH - 1, 7, c:c + 1],
                                         in1=root[:, :], op0=ALU.mult, op1=ALU.mult).then_inc(t_ok, 1)

        @block.tensor
        def _(pe):
            pe.wait_ge(const_dve, 3)
            pe.wait_ge(const_pool, 2)

            def sum_squares(n, acc=0):
                pe.wait_ge(sum_ok, n)
                pe.matmul(ps[:, 4, 0:T], ones[:, :], sq[:, acc, :], start=True, stop=True).then_inc(ss_ok, 1)

            with pe.Fori(0, DEPTH) as L:
                u0 = pe.snap(L * UNITS)
                e0 = pe.snap(L * EVACS)

                def product(out, j, col, rhs_hi, rhs_lo, first, last):
                    wh = w_hi[:, j % 2, col:col + P]
                    wl = w_lo[:, j % 2, col:col + P]
                    pe.matmul(out, wh, rhs_hi, start=first, stop=False)
                    pe.matmul(out, wh, rhs_lo, start=False, stop=False)
                    return pe.matmul(out, wl, rhs_hi, start=False, stop=last)

                def unit(q, j, evac_q, a_hi, a_lo):
                    pe.wait_ge(lo, u0 + q * 4 + (j + 1))
                    pe.wait_ge(evac, e0 + evac_q * 4 + (j + 1))
                    for c in range(C):
                        m = product(ps[:, j, 0:T], j, c * P, a_hi[:, c, :], a_lo[:, c, :], c == 0, c == C - 1)
                    m.then_inc(mm, 1)

                def segment(q_first, quads, a_hi=h_hi, a_lo=h_lo, skipped=0):
                    pe.sem_inc(passed, 1)
                    with pe.Fori(0, quads) as i:
                        for j in range(4):
                            unit(i + q_first, j, i + (q_first - skipped), a_hi, a_lo)

                def operand(n):
                    pe.wait_ge(op_lo, L * PREPS + n)

                def first_quad(q, n, skipped=0, a_hi=h_hi, a_lo=h_lo, squares=None,
                               order=range(C)):
                    for j in range(4):
                        pe.wait_ge(lo, u0 + (q * 4 + j + 1))
                        pe.wait_ge(evac, e0 + ((q - skipped) * 4 + j + 1))
                        for k, c in enumerate(order):
                            if j == 0:
                                operand(n + k + 1)
                            m = product(ps[:, j, 0:T], j, c * P, a_hi[:, c, :], a_lo[:, c, :], k == 0, k == C - 1)
                        m.then_inc(mm, 1)
                        if j == 1 and squares is not None:
                            sum_squares(L * NORMS + squares, order[0])

                first_quad(0, 0, squares=1)
                segment(1, 3)
                first_quad(4, C, a_hi=b_hi, a_lo=b_lo, squares=2)
                segment(5, 1, b_hi, b_lo)
                pe.wait_ge(t_ok, L * T_OPS + 2 * C)
                for k in range(3):
                    n = P if k < 2 else DEC
                    if k == 2:
                        pe.wait_ge(tok_ok, L * 3 + 1)
                    for c in range(C):
                        m = pe.transpose(ps[0:n, 4 + (2 * k + c // 4) % 4, c % 4 * P:c % 4 * P + P],
                                         t_op[:, c, k * P:k * P + n], ident[:, :])
                    m.then_inc(tr_ok, 1)
                segment(6, 2, b_hi, b_lo)
                pe.wait_ge(tok_ok, L * 3 + 3)
                pe.wait_ge(mixw_ok, L + 1)
                for g in range(GROUPS):
                    if g >= 4:
                        pe.wait_ge(s_used, L * GROUPS + (g - 3))
                    out = ps[:, 4 + g % 4, 0:T]
                    pe.matmul(out, ones[0:1, :], bias[0:1, g, :], start=True, stop=False)
                    for k in range(2):
                        pe.matmul(out[:, k * P:k * P + P], v_tok[:, k, g * P:g * P + P], ws[:, g, :],
                                  start=False, stop=False)
                    pe.matmul(out[:, SEQ:T], v_tok[0:DEC, 2, g * P:g * P + P], ws_blk[:, g, :],
                              start=False, stop=True).then_inc(s_ok, 1)
                segment(8, 6, b_hi, b_lo)
                operand(3 * C)
                segment(Q_A, 2)
                first_quad(Q_B, 3 * C, a_hi=b_hi, a_lo=b_lo)
                segment(Q_B + 1, 1, b_hi, b_lo)
                first_quad(Q_O, 4 * C)
                segment(Q_O + 1, 1)
                first_quad(Q_Q, 5 * C, a_hi=b_hi, a_lo=b_lo, squares=3)
                segment(Q_Q + 1, 3, b_hi, b_lo)
                pe.wait_ge(keys_got, L * 16 + 16)
                pe.wait_ge(evac, e0 + (4 + 4 * (Q_Q + 4)))
                for r in range(ROUTES):
                    g, tile, head = r // 2, r // HEADS, r % HEADS
                    if r % 2 == 0 and g >= 4:
                        pe.wait_ge(sc_in, L * (ROUTES // 2) + (g - 3))
                    for half in range(2):
                        at = r % 2 * 2 * KEYS + half * KEYS
                        m = pe.matmul(ps[0:TT, 4 + g % 4, at:at + KEYS],
                                      z[:, 2 * head + half, tile * TT:tile * TT + TT], keys[:, half, :],
                                      start=True, stop=True)
                    if r % 2:
                        m.then_inc(sc_ok, 1)
                operand(7 * C)
                def fine_segment(first, quads):
                    pe.sem_inc(passed, 1)
                    with pe.Fori(first, first + quads) as i:
                        for j in range(4):
                            pe.wait_ge(evac, e0 + i * 4 + (4 * Q_U + j + 1))
                            for c in range(C):
                                if c == 0:
                                    pe.wait_ge(lo_half, L * (N_FINE + 2) + i * 4 + (j + 1))
                                if c == C // 2:
                                    m.then_inc(mm_half, 1)
                                    pe.wait_ge(lo, u0 + i * 4 + (4 * Q_U + j + 1))
                                m = product(ps[:, j, 0:T], j, c * P, h_hi[:, c, :], h_lo[:, c, :],
                                            c == 0, c == C - 1)
                            m.then_inc(mm, 1)

                fine_segment(0, U_TOP + U_ONLY - 1)
                pe.wait_ge(rt_w, L + 1)
                for k in range(3):
                    for tile in range(NT):
                        m = pe.transpose(ps[:, 4 + k, tile * TT:tile * TT + TT],
                                         route[:, k, tile * HEADS:tile * HEADS + HEADS, :].rearrange("p r k -> p (r k)"),
                                         ident[0:TT, 0:TT])
                m.then_inc(rT_ok, 1)
                fine_segment(U_TOP + U_ONLY - 1, 1)
                with pe.Fori(0, U_MIX) as i:
                    groups_at = [5, 10, 16, 21, 26, 31]
                    done, k = 0, 0
                    for j in range(4):
                        pe.wait_ge(lo, u0 + i * 4 + (4 * (Q_U + U_TOP + U_ONLY) + j + 1))
                        pe.wait_ge(evac, e0 + i * 4 + (4 * (Q_U + U_TOP + U_ONLY) + j + 1))
                        for c in range(C):
                            m = product(ps[:, j, 0:T], j, c * P, h_hi[:, c, :], h_lo[:, c, :], c == 0, c == C - 1)
                            if c == C - 1:
                                m.then_inc(mm, 1)
                            done += 1
                            if done in groups_at:
                                pe.wait_ge(g_used, L * N_GROUPS + i * PER_QUAD + (k + 1))
                                for t in range(GROUP):
                                    if t % 2 == 0:
                                        pe.wait_ge(hot_ok, 2 * (L * N_GROUPS + i * PER_QUAD) + (2 * k + t // 2 + 1))
                                    m = pe.matmul(ps[:, 4 + k % 2, t * P:t * P + P], hot2[:, t, :], hot1[:, t, :],
                                                  start=True, stop=True)
                                    if t % 2 == 1:
                                        m.then_inc(g_ok, 1)
                                k += 1

                def expert_unit(q, j, e, first=False, last=False):
                    pe.wait_ge(lo, u0 + q * 4 + (j + 1))
                    pe.wait_ge(m_lo, L * KEYS + e + 1)
                    for c in range(C):
                        m = product(ps[:, c, 0:T], j, c * P, h_hi[:, j, :], h_lo[:, j, :], first, last)
                    m.then_inc(mm, 1)

                for j in range(4):
                    expert_unit(Q_V, j, j, first=(j == 0))
                with pe.Fori(1, KEYS // 4 - 1) as i:
                    for j in range(4):
                        expert_unit(i + Q_V, j, i * 4 + j)
                for j in range(4):
                    expert_unit(Q_PLE - 1, j, KEYS - 4 + j, last=(j == 3))

                operand(7 * C + CP)
                for j in range(4):
                    pe.wait_ge(lo, u0 + (4 * Q_PLE + j + 1))
                    if j < 2:
                        pe.wait_ge(x_up, L * X_UPS + (C + 2 + 2 * j))
                    else:
                        pe.wait_ge(evac, e0 + (4 * (Q_PLE - KEYS // 4) + j + 3))
                    for k in range(2):
                        for c in range(CP):
                            m = product(ps[:, 4 + (2 * j + k) % 4, 0:T], j, (k * CP + c) * P,
                                        h_hi[:, 4 + c, :], h_lo[:, 4 + c, :], c == 0, c == CP - 1)
                    m.then_inc(mm, 1)
                first_quad(Q_PG, 7 * C + CP, skipped=KEYS // 4, a_hi=b_hi, a_lo=b_lo, squares=4,
                           order=LATE_FIRST)
                segment(Q_PG + 1, 1, b_hi, b_lo, skipped=KEYS // 4)
            sum_squares(DEPTH * NORMS + 1)


def kernel(x_prompt, x_sample, state_conv, p_prompt, p_sample, ln1, w_in, ln_v, w_s, b_s, conv_w, w_a, w_b,
           w_o, ln2, w_q, k1, k2, u_tab, v_tab, ln3, w_pg, w_ple, ln_f):
    import numpy as np
    import concourse.bacc as bacc
    from concourse.bass_utils import run_bass_kernel_spmd

    def lay(a):
        return np.ascontiguousarray(np.asarray(a))

    def tiles(w):
        w = np.asarray(w)
        k, n = w.shape
        return w.reshape(k // P, P, n // P, P).transpose(2, 1, 0, 3).reshape(n // P, P, k)

    at = {n: i * 1024 for i, n in enumerate(["u", "v", "b", "c", "x", "ga", "gb"])}
    stream = np.empty((DEPTH * UNITS, P, D), np.float32)
    for l in range(DEPTH):
        parts = []
        wi = np.asarray(w_in[l])
        for n in SEGS:
            parts.append(tiles(wi[:, at[n]:at[n] + 1024]))
        for w in (w_a, w_b, w_o, w_q):
            parts.append(tiles(w[l]))
        parts.append(tiles(np.asarray(u_tab[l]).T))
        parts.append(np.asarray(v_tab[l]).reshape(KEYS, P, D))
        ple = np.zeros((4, P, D), np.float32)
        ple[:, :, 0:D // 2] = tiles(w_ple[l]).reshape(4, 2, P, CP * P).transpose(0, 2, 1, 3).reshape(4, P, D // 2)
        parts.append(ple)
        parts.append(tiles(w_pg[l]))
        k = l * UNITS
        for p in parts:
            stream[k:k + len(p)] = p
            k += len(p)
        assert k == (l + 1) * UNITS

    def tokens(prompt, sample):
        f = prompt.shape[-1]
        a = np.concatenate([np.asarray(prompt).reshape(SEQ, f), np.asarray(sample).reshape(DEC, f)])
        return lay(a.T.reshape(f // P, P, T).transpose(1, 0, 2))

    def per_feature(a):
        return np.asarray(a).reshape(C, P).T

    gains = np.empty((P, DEPTH, 8, C), np.float32)
    for l in range(DEPTH):
        for n, g in enumerate((ln1[l], ln_v[l], ln2[l], ln3[l], conv_w[l, 0], conv_w[l, 1], conv_w[l, 2],
                              ln1[l + 1] if l + 1 < DEPTH else ln_f)):
            gains[:, l, n, :] = per_feature(g)
    wsT = np.asarray(w_s).transpose(0, 3, 1, 2)
    bs = np.asarray(b_s)
    bias = np.concatenate([bs, bs] + [bs[:, :, 0:DEC_S]] * DEC_B, axis=2)
    keys = np.stack([np.asarray(k1).transpose(0, 2, 1), np.asarray(k2).transpose(0, 2, 1)], axis=2)
    conv = np.asarray(state_conv).reshape(DEPTH, DEC_B, 2, C, P).transpose(0, 4, 3, 1, 2)
    arrays = {
        "stream": stream,
        "x_in": tokens(x_prompt, x_sample),
        "pe_in": lay(np.stack([tokens(p_prompt[l], p_sample[l]) for l in range(DEPTH)])),
        "conv_in": lay(conv),
        "gains_in": gains,
        "ws_in": lay(wsT),
        "ws_blk_in": lay(wsT[:, 0:DEC_S, :, 0:DEC_S]),
        "bias_in": lay(bias),
        "keys_in": lay(keys),
    }
    nc = bacc.Bacc("TRN2", target_bir_lowering=False, num_devices=1)
    ins = [nc.dram_tensor(n, a.shape, F32, kind="ExternalInput").ap() for n, a in arrays.items()]
    shapes = {"y_out": (P, C, T), "conv_out": (DEPTH, P, C, 2 + 2 * DEC_B),
              "v_out": (DEPTH, P, C, DEC)}
    outs = [nc.dram_tensor(n, sh, F32, kind="ExternalOutput").ap() for n, sh in shapes.items()]
    hybrid_trunk(nc, *ins, *outs)
    got = run_bass_kernel_spmd(nc, [arrays], core_ids=[0]).results[0]
    y = got["y_out"].transpose(2, 1, 0).reshape(T, D)
    after = got["conv_out"]
    cp = after[:, :, :, 0:2].transpose(0, 3, 2, 1).reshape(DEPTH, 1, 2, D)
    cs = after[:, :, :, 2:].reshape(DEPTH, P, C, DEC_B, 2).transpose(0, 3, 4, 2, 1).reshape(DEPTH, DEC_B, 2, D)
    v = got["v_out"].transpose(0, 3, 2, 1).reshape(DEPTH, DEC_B, DEC_S, D)
    return (lay(y[0:SEQ].reshape(1, SEQ, D)), lay(y[SEQ:].reshape(DEC_B, DEC_S, D)), lay(cp), lay(cs), lay(v))
```
